# Optimizing a Trainium2 kernel written in Bass

```python
import jax
import jax.numpy as jnp
from jax import lax
import numpy as np
import jax, jax.numpy as jnp

D_MODEL = 1024
BATCH = 1
SEQ = 512
DEPTH = 1

HEAD_DIM = 64
ATTN_WIDTH = D_MODEL // 2
N_ATTN_HEADS = ATTN_WIDTH // HEAD_DIM
N_KV_HEADS = 2
KV_WIDTH = N_KV_HEADS * HEAD_DIM
WINDOW = 128
BLOCK = 128
ROPE_THETA = 500000.0
ROTARY_DIM = HEAD_DIM // 4
POOL_WINDOWS = (2, 4, 8, 16)
N_POOL_GROUPS = len(POOL_WINDOWS)
POOL_WIDTH = D_MODEL // 2
POOL_GROUP_WIDTH = POOL_WIDTH // N_POOL_GROUPS
MIX_WIDTH = ATTN_WIDTH + POOL_WIDTH
IN_WIDTH = ATTN_WIDTH + 2 * KV_WIDTH + POOL_WIDTH
D_FF = 2816
EPS = 1e-6


def rms_norm(x, g):
    xf = x.astype(jnp.float32)
    y = xf * lax.rsqrt(jnp.mean(xf * xf, axis=-1, keepdims=True) + EPS)
    return (y * g.astype(jnp.float32)).astype(x.dtype)

def swiglu(x, w_gate, w_up, w_down):
    return (jax.nn.silu(x @ w_gate) * (x @ w_up)) @ w_down

def rope_tables(positions):
    inv_freq = ROPE_THETA ** (-jnp.arange(0, ROTARY_DIM, 2, dtype=jnp.float32) / ROTARY_DIM)
    ang = positions.astype(jnp.float32)[:, None] * inv_freq[None, :]
    emb = jnp.concatenate([ang, ang], axis=-1)
    return jnp.cos(emb)[None, :, None, :], jnp.sin(emb)[None, :, None, :]

def apply_partial_rope(t, cos, sin):
    tf = t.astype(jnp.float32)
    rot, rest = tf[..., :ROTARY_DIM], tf[..., ROTARY_DIM:]
    half = ROTARY_DIM // 2
    rot_half = jnp.concatenate([-rot[..., half:], rot[..., :half]], axis=-1)
    rot = rot * cos + rot_half * sin
    return jnp.concatenate([rot, rest], axis=-1).astype(t.dtype)

def window_attention(q, k, v, sink):
    B, S, H, D = q.shape
    nb = S // BLOCK
    G = H // N_KV_HEADS
    qb = q.reshape(B, nb, BLOCK, N_KV_HEADS, G, D)

    def bands(t):
        tp = jnp.pad(t, ((0, 0), (BLOCK, BLOCK), (0, 0), (0, 0)))
        tb = tp.reshape(B, nb + 2, BLOCK, N_KV_HEADS, D)
        return jnp.concatenate([tb[:, :-2], tb[:, 1:-1], tb[:, 2:]], axis=2)

    kb, vb = bands(k), bands(v)
    scores = jnp.einsum('bnqkgd,bnskd->bnkgqs', qb, kb,
                        preferred_element_type=jnp.float32) * (D ** -0.5)
    qpos = jnp.arange(nb)[:, None] * BLOCK + jnp.arange(BLOCK)[None, :]
    kpos = jnp.arange(nb)[:, None] * BLOCK + jnp.arange(3 * BLOCK)[None, :] - BLOCK
    dist = qpos[:, :, None] - kpos[:, None, :]
    valid = (jnp.abs(dist) <= WINDOW) & (kpos[:, None, :] >= 0) & (kpos[:, None, :] < S)
    scores = jnp.where(valid[None, :, None, None], scores, -1e30)
    sink_l = sink.astype(jnp.float32).reshape(N_KV_HEADS, G)[None, None, :, :, None, None]
    m = jnp.maximum(jnp.max(scores, axis=-1, keepdims=True), sink_l)
    p = jnp.exp(scores - m)
    denom = jnp.sum(p, axis=-1, keepdims=True) + jnp.exp(sink_l - m)
    p = (p / denom).astype(v.dtype)
    out = jnp.einsum('bnkgqs,bnskd->bnqkgd', p, vb)
    return out.reshape(B, S, H * D)

def multiscale_pool(u, w_pool, pool_scale):
    B, S, _ = u.shape
    uf = u.astype(jnp.float32)
    csum = jnp.concatenate([jnp.zeros((B, 1, POOL_WIDTH), jnp.float32),
                            jnp.cumsum(uf, axis=1)], axis=1)
    t = jnp.arange(S)
    means = []
    for gi, w in enumerate(POOL_WINDOWS):
        cg = csum[..., gi * POOL_GROUP_WIDTH:(gi + 1) * POOL_GROUP_WIDTH]
        half = w // 2

        def win_mean(lo, hi):
            a = jnp.clip(lo, 0, S)
            b = jnp.clip(hi + 1, 0, S)
            s = jnp.take(cg, b, axis=1) - jnp.take(cg, a, axis=1)
            return s / (b - a).astype(jnp.float32)[None, :, None]

        means.append(0.5 * (win_mean(t - half, t + half - 1) + win_mean(t - half + 1, t + half)))
    mean = jnp.concatenate(means, axis=-1)
    d = (mean - uf).reshape(B, S, N_POOL_GROUPS, POOL_GROUP_WIDTH)
    y = jnp.einsum('bsgc,gcd->bsgd', d, w_pool.astype(jnp.float32)).reshape(B, S, POOL_WIDTH)
    return (y * pool_scale.astype(jnp.float32)).astype(u.dtype)

def first_inputs(seed: int = 0) -> dict:
    key = jax.random.key(seed)
    ks = jax.random.split(key, 18)
    f32 = jnp.float32
    L = DEPTH

    def nrm(k, shape, scale):
        return jax.random.normal(k, shape, f32) * scale

    def gain(k, shape, s=0.05):
        return 1.0 + s * jax.random.normal(k, shape, f32)

    return {
        'x': nrm(ks[0], (BATCH, SEQ, D_MODEL), 1.0),
        'ffn1_norm': gain(ks[1], (L, D_MODEL)),
        'ffn1_w_gate': nrm(ks[2], (L, D_MODEL, D_FF), D_MODEL ** -0.5),
        'ffn1_w_up': nrm(ks[3], (L, D_MODEL, D_FF), D_MODEL ** -0.5),
        'ffn1_w_down': nrm(ks[4], (L, D_FF, D_MODEL), D_FF ** -0.5),
        'mix_norm': gain(ks[5], (L, D_MODEL)),
        'w_in': nrm(ks[6], (L, D_MODEL, IN_WIDTH), D_MODEL ** -0.5),
        'sink_logits': nrm(ks[7], (L, N_ATTN_HEADS), 0.5),
        'pool_w': nrm(ks[8], (L, N_POOL_GROUPS, POOL_GROUP_WIDTH, POOL_GROUP_WIDTH), POOL_GROUP_WIDTH ** -0.5),
        'pool_scale': gain(ks[9], (L, POOL_WIDTH), 0.1),
        'w_out': nrm(ks[10], (L, MIX_WIDTH, D_MODEL), MIX_WIDTH ** -0.5),
        'ffn2_norm': gain(ks[11], (L, D_MODEL)),
        'ffn2_w_gate': nrm(ks[12], (L, D_MODEL, D_FF), D_MODEL ** -0.5),
        'ffn2_w_up': nrm(ks[13], (L, D_MODEL, D_FF), D_MODEL ** -0.5),
        'ffn2_w_down': nrm(ks[14], (L, D_FF, D_MODEL), D_FF ** -0.5),
        'final_norm': gain(ks[15], (D_MODEL,)),
    }

def first_block(x, ffn1_norm, ffn1_w_gate, ffn1_w_up, ffn1_w_down, mix_norm, w_in,
              sink_logits, pool_w, pool_scale, w_out, ffn2_norm, ffn2_w_gate,
              ffn2_w_up, ffn2_w_down, final_norm):
    B, S, _ = x.shape
    positions = jnp.arange(S, dtype=jnp.int32)
    cos, sin = rope_tables(positions)
    h = x
    for l in range(DEPTH):
        h = h + 0.5 * swiglu(rms_norm(h, ffn1_norm[l]), ffn1_w_gate[l], ffn1_w_up[l], ffn1_w_down[l])
        u = rms_norm(h, mix_norm[l]) @ w_in[l]
        q, k, v, pc = jnp.split(u, [ATTN_WIDTH, ATTN_WIDTH + KV_WIDTH, ATTN_WIDTH + 2 * KV_WIDTH], axis=-1)
        q = apply_partial_rope(q.reshape(B, S, N_ATTN_HEADS, HEAD_DIM), cos, sin)
        k = apply_partial_rope(k.reshape(B, S, N_KV_HEADS, HEAD_DIM), cos, sin)
        v = v.reshape(B, S, N_KV_HEADS, HEAD_DIM)
        a = window_attention(q, k, v, sink_logits[l])
        p = multiscale_pool(pc, pool_w[l], pool_scale[l])
        h = h + jnp.concatenate([a, p], axis=-1) @ w_out[l]
        h = h + 0.5 * swiglu(rms_norm(h, ffn2_norm[l]), ffn2_w_gate[l], ffn2_w_up[l], ffn2_w_down[l])
    return rms_norm(h, final_norm)


DEPTH_2 = 2

CHUNK = 64
ROPE_THETA_2 = 10000.0
A_Q_HEADS = (D_MODEL // 2) // HEAD_DIM
A_KV_HEADS = A_Q_HEADS // 4
A_WINDOW = 128
A_PREV_CHUNKS = A_WINDOW // CHUNK
B_KEY_DIM = 128
B_VAL_DIM = 128
B_HEADS = (D_MODEL // 2) // B_VAL_DIM
B_BLOCK = 32
C_HEADS = D_MODEL // HEAD_DIM
C_PREV_CHUNKS = 8
REL_CLIP = 128
CONV_WIDTH = 3
A_Q_DIM = A_Q_HEADS * HEAD_DIM
A_KV_DIM = A_KV_HEADS * HEAD_DIM
B_QK_DIM = B_HEADS * B_KEY_DIM
B_V_DIM = B_HEADS * B_VAL_DIM
EVEN_IN = A_Q_DIM + 2 * A_KV_DIM + 2 * B_QK_DIM + 2 * B_V_DIM
EVEN_MIX = A_Q_DIM + B_V_DIM
EVEN_SPLITS = (A_Q_DIM,
               A_Q_DIM + A_KV_DIM,
               A_Q_DIM + 2 * A_KV_DIM,
               A_Q_DIM + 2 * A_KV_DIM + B_QK_DIM,
               A_Q_DIM + 2 * A_KV_DIM + 2 * B_QK_DIM,
               A_Q_DIM + 2 * A_KV_DIM + 2 * B_QK_DIM + B_V_DIM)
C_DIM = C_HEADS * HEAD_DIM
ODD_IN = 3 * C_DIM
N_EVEN = (DEPTH_2 + 1) // 2
N_ODD = DEPTH_2 // 2


F32 = jnp.float32

def rms_norm_2(x, w):
    xf = x.astype(F32)
    y = xf * lax.rsqrt(jnp.mean(xf * xf, axis=-1, keepdims=True) + EPS)
    return (y * w.astype(F32)).astype(x.dtype)

def rope(x):
    S, D = x.shape[1], x.shape[3]
    inv_freq = ROPE_THETA_2 ** (-jnp.arange(0, D, 2, dtype=F32) / D)
    ang = jnp.arange(S, dtype=F32)[:, None] * inv_freq[None, :]
    cos = jnp.cos(ang)[None, :, None, :]
    sin = jnp.sin(ang)[None, :, None, :]
    xf = x.astype(F32)
    x1, x2 = xf[..., : D // 2], xf[..., D // 2:]
    return jnp.concatenate([x1 * cos - x2 * sin, x2 * cos + x1 * sin], axis=-1).astype(x.dtype)

def chunk_band_attention(q, k, v, n_prev, bias, sinks):
    B, S, Hq, D = q.shape
    Hkv = k.shape[2]
    G = Hq // Hkv
    n_chunks = S // CHUNK
    pad = n_prev * CHUNK
    band = pad + CHUNK
    scale = D ** -0.5
    k_pad = jnp.pad(k, ((0, 0), (pad, 0), (0, 0), (0, 0)))
    v_pad = jnp.pad(v, ((0, 0), (pad, 0), (0, 0), (0, 0)))
    qc = jnp.moveaxis(q.reshape(B, n_chunks, CHUNK, Hkv, G, D), 1, 0)
    key_idx = jnp.arange(band)

    def one_chunk(args):
        c, q_c = args
        start = c * CHUNK
        k_c = lax.dynamic_slice_in_dim(k_pad, start, band, axis=1)
        v_c = lax.dynamic_slice_in_dim(v_pad, start, band, axis=1)
        s = jnp.einsum('bqhgd,bjhd->bhgqj', q_c, k_c).astype(F32) * scale
        if bias is not None:
            s = s + bias.reshape(Hkv, G, CHUNK, band).astype(F32)
        valid = key_idx >= pad - start
        s = jnp.where(valid, s, -jnp.inf)
        if sinks is not None:
            sk = sinks.reshape(Hkv, G).astype(F32)[None, :, :, None, None]
            m = jnp.maximum(jnp.max(s, axis=-1, keepdims=True), sk)
            p = jnp.exp(s - m)
            p = p / (jnp.sum(p, axis=-1, keepdims=True) + jnp.exp(sk - m))
        else:
            p = jax.nn.softmax(s, axis=-1)
        o = jnp.einsum('bhgqj,bjhd->bqhgd', p.astype(v.dtype), v_c)
        return o.reshape(B, CHUNK, Hq, D)

    out = lax.map(one_chunk, (jnp.arange(n_chunks), qc))
    return jnp.moveaxis(out, 0, 1).reshape(B, S, Hq, D)

def hgrn2(q, f_logit, i, g, lb, norm_w):
    B, S, H, DK = q.shape
    DV = i.shape[-1]
    N = S // B_BLOCK
    lbh = lb.reshape(H, DK).astype(F32)
    f = lbh + (1.0 - lbh) * jax.nn.sigmoid(f_logit.astype(F32))
    log_f = jnp.log(f)
    k = 1.0 - f

    def blk(t):
        return t.reshape(B, N, B_BLOCK, H, t.shape[-1])

    qf, kf, vf, lf = blk(q.astype(F32)), blk(k), blk(i.astype(F32)), blk(log_f)
    cum = jnp.cumsum(lf, axis=2)
    last = cum[:, :, -1:]
    q_dec = qf * jnp.exp(cum)
    k_dec = kf * jnp.exp(-cum)
    k_end = kf * jnp.exp(last - cum)
    blk_decay = jnp.exp(last[:, :, 0])
    causal = jnp.tril(jnp.ones((B_BLOCK, B_BLOCK), dtype=bool))
    s = jnp.einsum('bnlhd,bnmhd->bnhlm', q_dec, k_dec)
    s = jnp.where(causal, s, 0.0)
    o_intra = jnp.einsum('bnhlm,bnmhe->bnlhe', s, vf)

    def step(state, xs):
        qd, ke, vv, dec = xs
        o = jnp.einsum('blhd,bhde->blhe', qd, state)
        state = dec[..., None] * state + jnp.einsum('blhd,blhe->bhde', ke, vv)
        return state, o

    state0 = jnp.zeros((B, H, DK, DV), F32)
    xs = (jnp.moveaxis(q_dec, 1, 0), jnp.moveaxis(k_end, 1, 0),
          jnp.moveaxis(vf, 1, 0), jnp.moveaxis(blk_decay, 1, 0))
    _, o_inter = lax.scan(step, state0, xs)
    o = (o_intra + jnp.moveaxis(o_inter, 0, 1)).reshape(B, S, H, DV)
    o = o * lax.rsqrt(jnp.mean(o * o, axis=-1, keepdims=True) + EPS) * norm_w.reshape(H, DV).astype(F32)
    return (o * jax.nn.silu(g.astype(F32))).astype(i.dtype)

def even_mixer(y, w_in, w_out, sinks, lb, gnorm_w):
    B, S, _ = y.shape
    proj = y @ w_in
    qa, ka, va, qb, fb, ib, gb = jnp.split(proj, EVEN_SPLITS, axis=-1)
    qa = rope(qa.reshape(B, S, A_Q_HEADS, HEAD_DIM))
    ka = rope(ka.reshape(B, S, A_KV_HEADS, HEAD_DIM))
    va = va.reshape(B, S, A_KV_HEADS, HEAD_DIM)
    oa = chunk_band_attention(qa, ka, va, A_PREV_CHUNKS, None, sinks)
    ob = hgrn2(qb.reshape(B, S, B_HEADS, B_KEY_DIM), fb.reshape(B, S, B_HEADS, B_KEY_DIM),
               ib.reshape(B, S, B_HEADS, B_VAL_DIM), gb.reshape(B, S, B_HEADS, B_VAL_DIM),
               lb, gnorm_w)
    o = jnp.concatenate([oa.reshape(B, S, A_Q_DIM), ob.reshape(B, S, B_V_DIM)], axis=-1)
    return o @ w_out

def odd_mixer(y, w_in, w_out, rel_table):
    B, S, _ = y.shape
    proj = y @ w_in
    q, k, v = jnp.split(proj, (C_DIM, 2 * C_DIM), axis=-1)
    q = q.reshape(B, S, C_HEADS, HEAD_DIM)
    k = k.reshape(B, S, C_HEADS, HEAD_DIM)
    v = v.reshape(B, S, C_HEADS, HEAD_DIM)
    pad = C_PREV_CHUNKS * CHUNK
    band = pad + CHUNK
    rel = jnp.arange(CHUNK)[:, None] + pad - jnp.arange(band)[None, :]
    idx = jnp.clip(rel, -REL_CLIP, REL_CLIP) + REL_CLIP
    bias = rel_table[:, idx]
    o = chunk_band_attention(q, k, v, C_PREV_CHUNKS, bias, None)
    return o.reshape(B, S, C_DIM) @ w_out

def conv_ffn(y, w_up, conv_w, conv_b, w_down):
    S = y.shape[1]
    up = y @ w_up
    u, v = jnp.split(up, 2, axis=-1)
    u_pad = jnp.pad(u, ((0, 0), (CONV_WIDTH - 1, 0), (0, 0)))
    c = conv_b
    for j in range(CONV_WIDTH):
        c = c + conv_w[j] * u_pad[:, j:j + S]
    return (jax.nn.gelu(c, approximate=False) * v) @ w_down

def second_inputs(seed: int = 0) -> dict:
    key = jax.random.key(seed)
    ks = jax.random.split(key, 16)
    nrm = jax.random.normal
    x = nrm(ks[0], (BATCH, SEQ, D_MODEL), F32)
    even_w_in = nrm(ks[1], (N_EVEN, D_MODEL, EVEN_IN), F32) * D_MODEL ** -0.5
    even_w_out = nrm(ks[2], (N_EVEN, EVEN_MIX, D_MODEL), F32) * EVEN_MIX ** -0.5
    even_sinks = nrm(ks[3], (N_EVEN, A_Q_HEADS), F32) * 0.5
    hgrn_lb_logits = nrm(ks[4], (N_EVEN + 1, B_QK_DIM), F32) * 0.1
    hgrn_norm_w = 1.0 + 0.02 * nrm(ks[5], (N_EVEN, B_V_DIM), F32)
    odd_w_in = nrm(ks[6], (N_ODD, D_MODEL, ODD_IN), F32) * D_MODEL ** -0.5
    odd_w_out = nrm(ks[7], (N_ODD, C_DIM, D_MODEL), F32) * C_DIM ** -0.5
    odd_rel_bias = nrm(ks[8], (N_ODD, C_HEADS, 2 * REL_CLIP + 1), F32) * 0.1
    ffn_w_up = nrm(ks[9], (DEPTH_2, D_MODEL, 2 * D_FF), F32) * D_MODEL ** -0.5
    ffn_conv_w = nrm(ks[10], (DEPTH_2, CONV_WIDTH, D_FF), F32) * CONV_WIDTH ** -0.5
    ffn_conv_b = nrm(ks[11], (DEPTH_2, D_FF), F32) * 0.02
    ffn_w_down = nrm(ks[12], (DEPTH_2, D_FF, D_MODEL), F32) * D_FF ** -0.5
    norm_w = 1.0 + 0.02 * nrm(ks[13], (DEPTH_2, 4, D_MODEL), F32)
    return {"x": x, "even_w_in": even_w_in, "even_w_out": even_w_out, "even_sinks": even_sinks,
            "hgrn_lb_logits": hgrn_lb_logits, "hgrn_norm_w": hgrn_norm_w,
            "odd_w_in": odd_w_in, "odd_w_out": odd_w_out, "odd_rel_bias": odd_rel_bias,
            "ffn_w_up": ffn_w_up, "ffn_conv_w": ffn_conv_w, "ffn_conv_b": ffn_conv_b,
            "ffn_w_down": ffn_w_down, "norm_w": norm_w}

def second_block(x, even_w_in, even_w_out, even_sinks, hgrn_lb_logits, hgrn_norm_w,
              odd_w_in, odd_w_out, odd_rel_bias, ffn_w_up, ffn_conv_w, ffn_conv_b,
              ffn_w_down, norm_w):
    lb_all = jnp.cumsum(jax.nn.softmax(hgrn_lb_logits.astype(F32), axis=0), axis=0)
    h = x
    for layer in range(DEPTH_2):
        nw = norm_w[layer]
        j = layer // 2
        y = rms_norm_2(h, nw[0])
        if layer % 2 == 0:
            y = even_mixer(y, even_w_in[j], even_w_out[j], even_sinks[j], lb_all[j], hgrn_norm_w[j])
        else:
            y = odd_mixer(y, odd_w_in[j], odd_w_out[j], odd_rel_bias[j])
        h = h + rms_norm_2(y, nw[1])
        y = conv_ffn(rms_norm_2(h, nw[2]), ffn_w_up[layer], ffn_conv_w[layer], ffn_conv_b[layer], ffn_w_down[layer])
        h = h + rms_norm_2(y, nw[3])
    return h


def setup_inputs(seed=0):
    out = dict(first_inputs(seed))
    for name, value in second_inputs(seed + 1).items():
        if name != "x":
            out[name + "_2"] = value
    return out


def reference(
    x, ffn1_norm, ffn1_w_gate, ffn1_w_up, ffn1_w_down, mix_norm, w_in, sink_logits, pool_w,
    pool_scale, w_out, ffn2_norm, ffn2_w_gate, ffn2_w_up, ffn2_w_down, final_norm, even_w_in_2,
    even_w_out_2, even_sinks_2, hgrn_lb_logits_2, hgrn_norm_w_2, odd_w_in_2, odd_w_out_2,
    odd_rel_bias_2, ffn_w_up_2, ffn_conv_w_2, ffn_conv_b_2, ffn_w_down_2, norm_w_2,
):
    x = first_block(
        x, ffn1_norm, ffn1_w_gate, ffn1_w_up, ffn1_w_down, mix_norm, w_in, sink_logits, pool_w,
        pool_scale, w_out, ffn2_norm, ffn2_w_gate, ffn2_w_up, ffn2_w_down, final_norm,
    )
    return second_block(
        x, even_w_in_2, even_w_out_2, even_sinks_2, hgrn_lb_logits_2, hgrn_norm_w_2, odd_w_in_2,
        odd_w_out_2, odd_rel_bias_2, ffn_w_up_2, ffn_conv_w_2, ffn_conv_b_2, ffn_w_down_2,
        norm_w_2,
    )


_drawn_inputs = setup_inputs


def setup_inputs(seed=0):
    import zlib

    import numpy as np

    out = dict(_drawn_inputs(seed))
    spreads = {}
    factors = {'sink_logits': 64.0, 'even_sinks_2': 64.0, 'hgrn_norm_w_2': 7.749, 'ffn_conv_b_2': 3.335}
    for name, (base, spread) in spreads.items():
        noise = np.random.default_rng([zlib.crc32(name.encode()), seed]).standard_normal(out[name].shape)
        drawn = base * np.exp(spread * noise) if base else spread * noise
        out[name] = jnp.asarray(drawn.astype(out[name].dtype))
    for name, factor in factors.items():
        out[name] = (out[name] * factor).astype(out[name].dtype)
    return out
```

```python
import concourse.bass as bass
import numpy as np
from concourse import mybir
from contextlib import ExitStack

F32 = mybir.dt.float32
F32R = mybir.dt.float32r
U32 = mybir.dt.uint32
ALU = mybir.AluOpType
ACT = mybir.ActivationFunctionType

P = 128
T = 512
D = 1024
KD = D // P
F = 2816
KF = F // P
NB = T // P
EPS = 1e-6
BIG = 1e30
HALF_TILES = (12, 10)
PAIR = 2 * KD * P
HGRN_BLOCK = 32
NHB = T // HGRN_BLOCK
POOL_WINDOWS = (2, 4, 8, 16)
PAD = 8
TAIL = 516

_VECS = [
    ("ffn1_norm", KD), ("mix_norm", KD), ("ffn2_norm", KD), ("final_norm", KD), ("norm_w_2", 8 * KD),
    ("ffn_conv_w_2", 2 * 3 * KF), ("ffn_conv_b_2", 2 * KF), ("pool_scale", 4), ("hgrn_norm_w_2", 4),
    ("hgrn_lb_logits_2", 8),
]
COL = {}
_c = 0
for _name, _n in _VECS:
    COL[_name] = _c
    _c += _n
NVEC = _c



class Stage:
    def __init__(self, name, kind, pairs, groups, evac):
        self.name, self.kind, self.pairs, self.groups, self.evac = name, kind, pairs, groups, evac


STAGES = [
    Stage("up1", "in", KF, KF, "silu"), Stage("down1", "down", 2 * KD, KD, "add"),
    Stage("in1", "in", 5, 5, "project"), Stage("out1", "in", KD // 2, KD // 2, "add"),
    Stage("up2", "in", KF, KF, "silu"), Stage("down2", "down", 2 * KD, KD, "add"),
    Stage("in2", "in", 11, 11, "project"), Stage("out2", "in", KD // 2, KD // 2, "hold"),
    Stage("up3", "in", KF, KF, "conv"), Stage("down3", "down", 2 * KD, KD, "hold"),
    Stage("in3", "in", 12, 12, "project"), Stage("out3", "in", KD // 2, KD // 2, "hold"),
    Stage("up4", "in", KF, KF, "conv"), Stage("down4", "down", 2 * KD, KD, "hold"),
]
_q = _g = 0
PAIR_TILES = []
for _s in STAGES:
    _s.q0, _s.g0 = _q, _g
    _q += _s.pairs
    _g += _s.groups
    PAIR_TILES += [2 * KD] * _s.pairs if _s.kind == "in" else list(HALF_TILES) * KD
NPAIR = _q
BY = {s.name: s for s in STAGES}
for _n, _x, _r in (("up1", 0, 0), ("in1", 1, 1), ("up2", 2, 2), ("in2", 3, 4), ("up3", 4, 6), ("in3", 5, 8), ("up4", 6, 10)):
    BY[_n].x_index, BY[_n].stat = _x, _r
for _n, _x, _r, _v, _f in (("down1", 1, 1, "mix_norm", 0.5), ("out1", 2, 2, "ffn2_norm", 1.0), ("down2", None, 3, None, 0.5),
                           ("out2", None, 5, None, 1.0), ("down3", None, 7, None, 1.0), ("out3", None, 9, None, 1.0),
                           ("down4", None, 11, None, 1.0)):
    BY[_n].x_index, BY[_n].stat, BY[_n].next_norm, BY[_n].factor = _x, _r, (COL[_v] if _v else None), _f
NW = COL["norm_w_2"]
BARRIERS = {
    "down2": dict(kind="final", col=COL["final_norm"], next_col=NW + 0 * KD, x_index=3, stat=4, h0=0),
    "out2": dict(kind="post", col=NW + 1 * KD, next_col=NW + 2 * KD, x_index=4, stat=6, h0=8),
    "down3": dict(kind="post", col=NW + 3 * KD, next_col=NW + 4 * KD, x_index=5, stat=8, h0=16),
    "out3": dict(kind="post", col=NW + 5 * KD, next_col=NW + 6 * KD, x_index=6, stat=10, h0=24),
    "down4": dict(kind="post", col=NW + 7 * KD, next_col=None, x_index=None, stat=None, h0=32),
}
ATTENTIONS = [
    dict(heads=8, grouped=True, back=1, ahead=1, q=0, k=4, v=5),
    dict(heads=8, grouped=True, back=1, ahead=0, q=0, k=4, v=5),
    dict(heads=16, grouped=False, back=NB, ahead=0, q=0, k=8, v=16),
]
for _i, _a in enumerate(ATTENTIONS):
    _a["units"] = []
    for _h in range(_a["heads"]):
        for _n in range(NB):
            _lo, _hi = max(0, _n - _a["back"]), min(NB - 1, _n + _a["ahead"])
            _a["units"].append((_h // 2, _h % 2, _n, _lo, _hi - _lo + 1))
    _a["u0"] = sum(len(b["units"]) for b in ATTENTIONS[:_i])


def wait(eng, sem, count):
    if not isinstance(count, int) or count > 0:
        eng.wait_ge(sem, count)


def chunk(t, m, width=T):
    if isinstance(m, int):
        return t[:, m * width:(m + 1) * width]
    return t[:, bass.ds(m * width, width)]


def column(t, c):
    return t[:, c:c + 1] if isinstance(c, int) else t[:, bass.ds(c, 1)]


def repeat(eng, n, body, first=0, last=0):
    first = min(first, n)
    last = min(last, n - first)
    for i in range(first):
        body(i)
    middle = n - first - last
    if middle == 1:
        body(first)
    elif middle > 1:
        with eng.Fori(first, n - last) as i:
            body(i)
    for i in range(n - last, n):
        body(i)


def build(nc, x_t, vecs, weights, mixer_consts, pool_tab, small_consts, pool_w, sinks, rel_bias, out_t, scratch, skew, stop=None):
    names = [s.name for s in STAGES]
    stages = STAGES if stop is None else STAGES[:names.index(stop) + 1]
    last_pair = stages[-1].q0 + stages[-1].pairs

    with ExitStack() as ctx:
        base = nc.sbuf_base
        place = [(base + 31) // 32 * 32]
        SLOT = T * 4

        def at(name, shape, dt, offset):
            return nc.alloc_sbuf_tensor_at(name, shape, dt, offset=offset)

        def new(name, words, dt=F32):
            t = at(name, [P, words], dt, place[0])
            place[0] += (words * 4 + 31) // 32 * 32
            return t

        def sem(name):
            return ctx.enter_context(nc.semaphore(name))

        act_at = place[0]
        act = new("act", 2 * KF * T, F32R)
        x_at = place[0]
        x_split = new("x_split", 2 * KD * T, F32R)
        h = new("h", KD * T)
        raw = new("raw", 2 * PAIR)
        w_hi = new("w_hi", 2 * PAIR, F32R)
        w_lo = new("w_lo", 2 * PAIR, F32R)
        gate = new("gate", T)
        gated = new("gated", T)
        up = new("up", T)
        prod = new("prod", T)
        shifted = new("shifted", T + 2)
        sq = new("sq", 2 * T)
        ssum = new("ssum", T)
        rstd = new("rstd", T)
        vec = new("vec", NVEC)
        small = new("small", 3 * P)
        lbs = new("lbs", 32)
        tiny = new("tiny", 256)
        arena_words = (place[0] - base + 3) // 4
        ctx.enter_context(nc.sbuf_tensor("arena", [P, arena_words], F32))
        std = sq
        ident, mean_d, mean_head = small[:, 0:P], small[:, P:2 * P], small[:, 2 * P:3 * P]

        proj = at("proj", [P, 24 * T], F32, act_at)
        mconst = at("mconst", [P, 4 * T], F32, act_at + 24 * SLOT)
        mix_hi = act[:, 28 * T:36 * T]
        mix_lo = act[:, 36 * T:44 * T]
        cos, sin = mconst[:, 0:T], mconst[:, T:2 * T]
        mask = mconst[:, 2 * T:2 * T + 384]
        perm = mconst[:, 2 * T + 384:3 * T]
        pick = [mconst[:, 3 * T + g * P:3 * T + (g + 1) * P] for g in range(2)]
        pick_perm = [mconst[:, 3 * T + (2 + g) * P:3 * T + (3 + g) * P] for g in range(2)]
        y = at("y", [P, KD * T], F32, x_at)
        xs = lambda n, words, k: at(n, [P, words], F32, x_at + k * SLOT)
        rot_a, rot_b = xs("rot_a", T, 0), xs("rot_b", T, 1)
        kdup = xs("kdup", 2 * T, 2)
        v_tok = xs("v_tok", 2 * T, 4)
        spare = [xs(f"spare{k}", T, k) for k in (0, 1, 14, 15)]
        near = [xs(f"near{k}", T, k) for k in range(6, 12)]
        score = [near[:2] + [spare[s]] for s in (2, 2, 0)]
        prob = [near[2:] + [spare[s]] for s in (3, 3, 1)]
        prob_t = xs("prob_t", 2 * T, 12)
        biases = xs("biases", 2 * T, 14)
        up_at = lambda n, words, k: at(n, [P, words], F32, act_at + k * SLOT)
        pw = up_at("pw", 4 * P, 11)
        pool_d = [up_at(f"pool_d{g}", T, k) for g, k in enumerate((10, 12, 13, 23))]
        ptab = up_at("ptab", 4 * TAIL, 14)
        csum = up_at("csum", T + 1 + 2 * PAD, 19)
        pool_e = up_at("pool_e", T + 1, 21)
        hk, he = xs("hk", 4 * T, 0), xs("he", 4 * T, 4)
        hkd, hc = xs("hkd", 4 * T, 8), xs("hc", 4 * T, 12)
        state = [up_at("state0", 4 * T, 0), up_at("state1", 4 * T, 10)]
        s_t = up_at("s_t", 2 * T, 4)
        osq = up_at("osq", T, 22)
        reset = up_at("reset", T, 23)
        hq, hf, hv, hg = (proj[:, k * T:(k + 4) * T] for k in (6, 10, 14, 18))

        ps = ctx.enter_context(nc.psum_tensor("ps", [P, 8 * T], F32))
        bank = lambda b, n=1: ps[:, b * T:(b + n) * T]
        STATS_BANK = 4

        raw_landed = [sem(f"raw_landed{k}") for k in range(2)]
        x_landed = sem("x_landed")
        vec_landed = sem("vec_landed")
        hi_rounded = sem("hi_rounded")
        lo_rounded = sem("lo_rounded")
        pair_done = sem("pair_done")
        evacuated = sem("evacuated")
        gate_ready = sem("gate_ready")
        gated_ready = sem("gated_ready")
        prod_ready = sem("prod_ready")
        prod_hi = sem("prod_hi")
        act_ready = sem("act_ready")
        u_ready = sem("u_ready")
        conv_a = sem("conv_a")
        conv_b = sem("conv_b")
        x_hi_ready = sem("x_hi_ready")
        x_ready = sem("x_ready")
        sq_ready = sem("sq_ready")
        ssum_ready = sem("ssum_ready")
        ms_ready = sem("ms_ready")
        std_ready = sem("std_ready")
        rstd_ready = sem("rstd_ready")
        h_ready = sem("h_ready")
        scaled_ready = sem("scaled_ready")
        mix_hi_ready = sem("mix_hi_ready")
        mix_ready = sem("mix_ready")
        out_landed = sem("out_landed")
        dve_step = sem("dve_step")
        act_step = sem("act_step")
        pool_step = sem("pool_step")
        const_landed = sem("const_landed")
        tab_landed = sem("tab_landed")
        sink_landed = sem("sink_landed")
        rope_ps = sem("rope_ps")
        rope_done = sem("rope_done")
        kdup_done = sem("kdup_done")
        v_ps = sem("v_ps")
        v_done = sem("v_done")
        scores_ps = sem("scores_ps")
        neg_max = sem("neg_max")
        probs = sem("probs")
        probs_t_ps = sem("probs_t_ps")
        probs_normed = sem("probs_normed")
        probs_t = sem("probs_t")
        weighed = sem("weighed")
        far_ready = sem("far_ready")
        csum_done = sem("csum_done")
        csum_used = sem("csum_used")
        pool_diff = sem("pool_diff")
        pool_ps = sem("pool_ps")
        bias_landed = [sem(f"bias_landed{k}") for k in range(2)]
        bias_scaled = sem("bias_scaled")
        bias_ready = sem("bias_ready")
        table_landed = sem("table_landed")
        hg_sig = sem("hg_sig")
        hg_lb = sem("hg_lb")
        lb_ready = sem("lb_ready")
        hg_tb = sem("hg_tb")
        hg_f = sem("hg_f")
        hg_ln = sem("hg_ln")
        hg_cum = sem("hg_cum")
        hg_exp = sem("hg_exp")
        hg_diff = sem("hg_diff")
        hg_kend = sem("hg_kend")
        hg_q = sem("hg_q")
        hg_tp = sem("hg_tp")
        hg_ta = sem("hg_ta")
        hg_s_ps = sem("hg_s_ps")
        hg_s = sem("hg_s")
        hg_u_ps = sem("hg_u_ps")
        hg_state = sem("hg_state")
        hg_o = sem("hg_o")
        hg_osq = sem("hg_osq")
        hg_ms = sem("hg_ms")
        hg_std = sem("hg_std")
        hg_norm = sem("hg_norm")

        NEG, ROW, INV = (tiny[:, 16 * k:16 * (k + 1)] for k in range(3))
        sink_col, neg_sink, decay = tiny[:, 80:96], tiny[:, 96:112], tiny[:, 128:192]
        lb_m, lb_e, lb_s, lb, lb_rest = (tiny[:, 192 + 8 * k:200 + 8 * k] for k in range(5))
        IN = ("in1", "in2", "in3")
        LAG_N, LAG_T, LAG_V, LAG_MIX, AHEAD = 2, 4, 5, 6, 6

        def projected(a):
            s = BY[IN[a]]
            return s.g0 + s.groups

        def stat_col(c, hh, n):
            k = 8 * (c % 2) + 4 * hh + n
            return slice(k, k + 1)

        def key_bias(a, c, hh, n, lo, nk):
            if a < 2:
                off = (lo - (n - 1)) * P
                return mask[:, off:off + nk * P]
            off = hh * T + (NB - 1 - n) * P
            return biases[:, off:off + nk * P]

        def attention_pe(pe, a):
            at_, units = ATTENTIONS[a], ATTENTIONS[a]["units"]
            u0, nc_ = at_["u0"], at_["heads"] // 2
            pe.wait_ge(evacuated, projected(a))
            pe.wait_ge(const_landed, 16 * (a + 1))

            def values(c):
                b = 3 if a < 2 else 7
                src = at_["v"] + (c if a == 2 else 0)
                for n in range(NB):
                    ins = pe.transpose(bank(b)[:, n * P:(n + 1) * P], proj[:, src * T + n * P:src * T + (n + 1) * P], ident)
                ins.then_inc(v_ps, 1)

            def rotate(c):
                pe.matmul(bank(7), perm, chunk(proj, at_["q"] + c), start=True, stop=True).then_inc(rope_ps, 1)

            if a < 2:
                for g in range(2):
                    pe.matmul(bank(7 - 2 * g), pick[g], chunk(proj, at_["k"]), start=True, stop=True)
                    pe.matmul(bank(6 - 2 * g), pick_perm[g], chunk(proj, at_["k"]), start=True, stop=True).then_inc(rope_ps, 1)
                values(0)
                pe.wait_ge(kdup_done, 2 * a + 1)
                rotate(0)
                pe.wait_ge(v_done, a + 1)
            else:
                values(0)
            for step in range(len(units) + LAG_MIX + 1):
                if step < len(units):
                    c, hh, n, lo, nk = units[step]
                    if hh == 0 and n == 0 and a < 2:
                        pe.wait_ge(rope_done, 4 * a + c + 1)
                        pe.wait_ge(kdup_done, 2 * a + 2)
                    if step >= 3:
                        pe.wait_ge(neg_max, u0 + step - 2)
                    rows = slice(64 * hh, 64 * hh + 64)
                    if a < 2:
                        k_ap = kdup[rows, (c // 2) * T + lo * P:(c // 2) * T + (lo + nk) * P]
                    else:
                        k_ap = proj[rows, (at_["k"] + c) * T + lo * P:(at_["k"] + c) * T + (lo + nk) * P]
                    qs = (at_["q"] + c) * T + n * P
                    pe.matmul(bank(step % 3)[:, 0:nk * P], proj[rows, qs:qs + P], k_ap, start=True, stop=True)\
                        .then_inc(scores_ps, 1)
                u = step - LAG_T
                if 0 <= u < len(units):
                    nk = units[u][4]
                    pe.wait_ge(probs_normed, u0 + u + 1)
                    if u >= 2:
                        pe.wait_ge(probs_t, u0 + u - 1)
                    for j in range(nk):
                        ins = pe.transpose(bank(3 + u % 2)[:, j * P:(j + 1) * P], prob[a][u % 5][:, j * P:(j + 1) * P], ident)
                    ins.then_inc(probs_t_ps, 1)
                u = step - LAG_V
                if 0 <= u < len(units):
                    c, hh, n, lo, nk = units[u]
                    if hh == 0 and n == 0:
                        if c >= 2:
                            pe.wait_ge(mix_ready, KD * a + c - 1)
                        if a == 2:
                            pe.wait_ge(v_done, 2 + c + 1)
                    pe.wait_ge(probs_t, u0 + u + 1)
                    for j in range(nk):
                        vc = (lo + j) * P + (64 * (c // 2) if a < 2 else (c % 2) * T + 64 * hh)
                        ins = pe.matmul(bank(5 + c % 2)[64 * hh:64 * hh + 64, n * P:(n + 1) * P], v_tok[:, vc:vc + 64],
                                        prob_t[:, (u % 2) * T + j * P:(u % 2) * T + (j + 1) * P], start=j == 0, stop=j == nk - 1)
                    ins.then_inc(weighed, 1)
                c, e = divmod(step - AHEAD, 8)
                if e == 0 and 0 <= c < nc_ - 1:
                    if a < 2:
                        rotate(c + 1)
                    else:
                        values(c + 1)
            if a == 0:
                pe.wait_ge(mix_ready, nc_)
                pe.wait_ge(tab_landed, 32)
                for g in range(4):
                    pe.wait_ge(pool_diff, g + 1)
                    pe.matmul(bank(4 + g), pw[:, g * P:(g + 1) * P], pool_d[g][:, :], start=True, stop=True).then_inc(pool_ps, 1)

        def attention_act(eng, a):
            at_, units = ATTENTIONS[a], ATTENTIONS[a]["units"]
            u0, nc_ = at_["u0"], at_["heads"] // 2

            def values(c):
                eng.wait_ge(v_ps, (a if a < 2 else 2 + c) + 1)
                if a == 2 and c >= 2:
                    eng.wait_ge(weighed, u0 + 8 * (c - 1))
                eng.activation(chunk(v_tok, c % 2 if a == 2 else 0), bank(7 if a == 2 else 3), ACT.Copy).then_inc(v_done, 1)

            values(0)
            for step in range(len(units) + LAG_MIX + 1):
                u = step - LAG_T
                if 0 <= u < len(units):
                    eng.wait_ge(probs_t_ps, u0 + u + 1)
                    if u >= 2:
                        eng.wait_ge(weighed, u0 + u - 1)
                    w = units[u][4] * P
                    eng.activation(prob_t[:, (u % 2) * T:(u % 2) * T + w], bank(3 + u % 2)[:, 0:w], ACT.Copy).then_inc(probs_t, 1)
                if step < len(units):
                    c, hh, n, lo, nk = units[step]
                    k = stat_col(c, hh, n)
                    w = nk * P + (a < 2)
                    eng.wait_ge(neg_max, u0 + step + 1)
                    if step >= 5:
                        eng.wait_ge(probs_t_ps, u0 + step - 4)
                    eng.activation(prob[a][step % 5][:, 0:w], score[a][step % 3][:, 0:w],
                                   ACT.Exp, bias=NEG[:, k], scale=-1.0, accum_out=ROW[:, k]).then_inc(probs, 1)
                c, e = divmod(step - 7 - LAG_MIX, 8)
                if e == 0 and 0 <= c < nc_:
                    eng.wait_ge(weighed, u0 + 8 * c + 8)
                    eng.activation(chunk(mix_hi, c), bank(5 + c % 2), ACT.Copy).then_inc(mix_hi_ready, 1)
                c, e = divmod(step - AHEAD, 8)
                if e == 0 and 0 <= c < nc_ - 1 and a == 2:
                    values(c + 1)
            if a == 0:
                for g in range(4):
                    eng.wait_ge(pool_ps, g + 1)
                    eng.activation(chunk(mix_hi, 4 + g), bank(4 + g), ACT.Copy, scale=column(vec, COL["pool_scale"] + g))\
                        .then_inc(mix_hi_ready, 1)

        def attention_dve(eng, a, link):
            at_, units = ATTENTIONS[a], ATTENTIONS[a]["units"]
            u0, nc_ = at_["u0"], at_["heads"] // 2
            eng.wait_ge(evacuated, projected(a))
            eng.wait_ge(const_landed, 16 * (a + 1))
            if a == 0:
                eng.wait_ge(sink_landed, 16)
                link(eng.tensor_scalar(neg_sink, sink_col, -1.0, None, ALU.mult))
                eng.memset(gate[:, :], 1.0)
                link(eng.memset(csum[:, 0:PAD + 1], 0.0))

            def rotated(out, plain, turned, done, count):
                link(eng.tensor_tensor(rot_a[:, :], plain, cos, ALU.mult))
                link(eng.tensor_tensor(rot_b[:, :], turned, sin, ALU.mult))
                eng.tensor_tensor(out, rot_a[:, :], rot_b[:, :], ALU.add).then_inc(done, 1)
                eng.wait_ge(done, count)

            def rotate(c):
                eng.wait_ge(rope_ps, 6 * a + 2 + c + 1)
                rotated(chunk(proj, at_["q"] + c), chunk(proj, at_["q"] + c), bank(7), rope_done, 4 * a + c + 1)

            def window_sums(g):
                if g:
                    eng.wait_ge(csum_used, g)
                u = chunk(proj, 6 + g)
                link(eng.tensor_tensor_scan(csum[:, PAD + 1:PAD + 1 + T], gate[:, :], u, 0.0, ALU.mult, ALU.add))
                eng.tensor_copy(csum[:, PAD + 1 + T:], csum[:, PAD + T:PAD + T + 1].to_broadcast([P, PAD])).then_inc(csum_done, 1)

            if a < 2:
                for g in range(2):
                    eng.wait_ge(rope_ps, 6 * a + g + 1)
                    rotated(chunk(kdup, g), bank(7 - 2 * g), bank(6 - 2 * g), kdup_done, 2 * a + g + 1)
                rotate(0)
            for step in range(len(units) + LAG_MIX + 1):
                u = step - LAG_N
                if 0 <= u < len(units):
                    c, hh, n, lo, nk = units[u]
                    k = stat_col(c, hh, n)
                    eng.wait_ge(probs, u0 + u + 1)
                    link(eng.reciprocal(INV[:, k], ROW[:, k]))
                    p = prob[a][u % 5][:, 0:nk * P]
                    eng.tensor_scalar(p, p, INV[:, k], None, ALU.mult).then_inc(probs_normed, 1)
                if step < len(units):
                    c, hh, n, lo, nk = units[step]
                    k = stat_col(c, hh, n)
                    eng.wait_ge(scores_ps, u0 + step + 1)
                    if step >= 3:
                        eng.wait_ge(probs, u0 + step - 2)
                    if a == 2 and n == 0:
                        eng.wait_ge(bias_ready, 2 * c + hh + 1)
                    s = 8 * a + 2 * c + hh
                    if a < 2:
                        eng.tensor_copy(score[a][step % 3][:, nk * P:nk * P + 1], neg_sink[:, s:s + 1])
                    eng.tensor_tensor_reduce(out=score[a][step % 3][:, 0:nk * P], in0=bank(step % 3)[:, 0:nk * P],
                                             in1=key_bias(a, c, hh, n, lo, nk), scale=-0.125,
                                             scalar=neg_sink[:, s:s + 1] if a < 2 else 3e38, op0=ALU.add, op1=ALU.min,
                                             accum_out=NEG[:, k]).then_inc(neg_max, 1)
                c, e = divmod(step - 7 - LAG_MIX, 8)
                if e == 0 and 0 <= c < nc_:
                    eng.wait_ge(mix_hi_ready, KD * a + c + 1)
                    eng.tensor_tensor(chunk(mix_lo, c), bank(5 + c % 2), chunk(mix_hi, c).bitcast(F32), ALU.subtract)\
                        .then_inc(mix_ready, 1)
                c, e = divmod(step - AHEAD, 8)
                if e == 0 and 0 <= c < nc_ - 1 and a < 2:
                    rotate(c + 1)
                if a == 0 and step % 8 == 2 and step // 8 < 4:
                    window_sums(step // 8)
            if a == 0:
                for g in range(4):
                    eng.wait_ge(mix_hi_ready, 4 + g + 1)
                    eng.scalar_tensor_tensor(chunk(mix_lo, 4 + g), bank(4 + g), column(vec, COL["pool_scale"] + g),
                                             chunk(mix_hi, 4 + g).bitcast(F32), ALU.mult, ALU.subtract).then_inc(mix_ready, 1)

        def pool_gpsimd(eng):
            for g, w in enumerate(POOL_WINDOWS):
                half = w // 2
                eng.wait_ge(csum_done, g + 1)
                eng.wait_ge(tab_landed, 32)
                eng.tensor_tensor(pool_e[:, :], csum[:, PAD + half:PAD + half + T + 1], csum[:, PAD - half:PAD - half + T + 1],
                                  ALU.subtract).then_inc(csum_used, 1)
                eng.wait_ge(csum_used, g + 1)
                eng.tensor_tensor(pool_e[:, :], pool_e[:, :], ptab[:, g * TAIL:g * TAIL + T + 1], ALU.mult).then_inc(pool_step, 1)
                eng.wait_ge(pool_step, 2 * g + 1)
                eng.tensor_tensor(pool_d[g][:, :], pool_e[:, 0:T], pool_e[:, 1:T + 1], ALU.add).then_inc(pool_step, 1)
                eng.wait_ge(pool_step, 2 * g + 2)
                eng.tensor_tensor(pool_d[g][:, :], pool_d[g][:, :], chunk(proj, 6 + g), ALU.subtract).then_inc(pool_diff, 1)

        def skewed(hd):
            return skew[hd, 0:5 * P * P].rearrange("(p w) -> p w", w=5 * P)[:, P - 1:P - 1 + T]

        def bias_gpsimd(eng):
            for hd in range(16):
                k = hd % 2
                if hd == 0:
                    eng.wait_ge(table_landed, 64)
                    eng.wait_ge(pair_done, BY["in3"].q0 + BY["in3"].pairs)
                if hd >= 2:
                    eng.wait_ge(neg_max, ATTENTIONS[2]["u0"] + 4 * (hd - 1))
                eng.dma_start(chunk(biases, k), skewed(hd))\
                    .then_inc(bias_landed[k], 16)
                eng.wait_ge(bias_landed[k], 16 * (hd // 2 + 1))
                eng.tensor_scalar(chunk(biases, k), chunk(biases, k), 8.0, None, ALU.mult).then_inc(bias_scaled, 1)
                eng.wait_ge(bias_scaled, hd + 1)
                own = biases[:, k * T + 3 * P:(k + 1) * T]
                eng.tensor_tensor(own, own, mask[:, 0:P], ALU.add).then_inc(bias_ready, 1)

        def state_col(b):
            return slice((b - 1) * P, b * P)

        def hgrn_pe(pe):
            a0 = 4 * (NHB - 1)
            for hd in range(4):
                for n in range(NB):
                    ins = pe.transpose(bank(hd)[:, n * P:(n + 1) * P], hv[:, hd * T + n * P:hd * T + (n + 1) * P], ident)
                ins.then_inc(hg_tp, 1)
            pe.wait_ge(hg_kend, 1)
            pe.wait_ge(mix_ready, KD + 4)
            for hd in range(4):
                for n in range(NB):
                    ins = pe.transpose(bank(4 + hd)[:, n * P:(n + 1) * P], hc[:, hd * T + n * P:hd * T + (n + 1) * P], ident)
                ins.then_inc(hg_tp, 1)
            pe.wait_ge(hg_ta, 4)
            pe.wait_ge(hg_tb, 4)
            pe.wait_ge(hg_q, 3)

            def mean_square(hd):
                pe.wait_ge(hg_osq, hd + 1)
                if hd:
                    pe.wait_ge(hg_std, hd)
                pe.matmul(bank(7), mean_head, osq[:, :], start=True, stop=True).then_inc(hg_ms, 1)

            for hd in range(4):
                o = bank(5 + hd % 2)
                if hd:
                    pe.wait_ge(hg_s, hd)
                for n in range(NB):
                    w = slice(hd * T + n * P, hd * T + (n + 1) * P)
                    ins = pe.matmul(bank(0)[:, n * P:(n + 1) * P], hkd[:, w], hq[:, w], start=True, stop=True)
                ins.then_inc(hg_s_ps, 1)
                if hd:
                    pe.wait_ge(hg_state, (NHB - 1) * hd)
                for b in range(NHB - 1):
                    grp, r = divmod(b, 4)
                    w = slice(hd * T + grp * P, hd * T + (grp + 1) * P)
                    rows = slice(32 * r, 32 * r + 32)
                    ins = pe.matmul(bank(1 + r)[:, grp * P:(grp + 1) * P], hk[rows, w], he[rows, w], start=True, stop=True)
                ins.then_inc(hg_u_ps, 1)
                if hd:
                    mean_square(hd - 1)
                pe.wait_ge(hg_s, hd + 1)
                if hd >= 2:
                    pe.wait_ge(hg_norm, hd - 1)
                for n in range(NB):
                    pe.matmul(o[:, n * P:(n + 1) * P], he[:, hd * T + n * P:hd * T + (n + 1) * P],
                              s_t[:, (hd % 2) * T + n * P:(hd % 2) * T + (n + 1) * P], start=n == 0, stop=False,
                              skip_group_check=True)
                for b in range(1, NHB):
                    pe.wait_ge(hg_state, (NHB - 1) * hd + b)
                    w = slice(b * HGRN_BLOCK, (b + 1) * HGRN_BLOCK)
                    ins = pe.matmul(o[:, w], state[hd % 2][:, state_col(b)], chunk(hq, hd)[:, w], start=False,
                                    stop=b == NHB - 1, skip_group_check=True)
                ins.then_inc(hg_o, 1)
            mean_square(3)

        def hgrn_act(eng):
            eng.wait_ge(lb_ready, 1)
            eng.activation(lb_e, lb_m, ACT.Exp).then_inc(hg_lb, 1)
            eng.wait_ge(mix_ready, KD + 4)
            eng.activation(hk[:, :], hf, ACT.Sigmoid).then_inc(hg_sig, 1)
            eng.activation(hg, hg, ACT.Silu).then_inc(hg_sig, 1)
            eng.wait_ge(hg_f, 2)
            eng.activation(hf, hf, ACT.Ln).then_inc(hg_ln, 1)
            eng.wait_ge(hg_cum, 1)
            eng.activation(he[:, :], hc[:, :], ACT.Exp).then_inc(hg_exp, 1)
            eng.activation(hkd[:, :], hc[:, :], ACT.Exp, scale=-1.0).then_inc(hg_exp, 1)
            eng.wait_ge(hg_diff, 1)
            eng.activation(hf, hf, ACT.Exp).then_inc(hg_exp, 1)
            eng.wait_ge(hg_q, 2)
            for hd in range(4):
                eng.wait_ge(hg_tp, hd + 1)
                eng.activation(chunk(he, hd), bank(hd), ACT.Copy).then_inc(hg_ta, 1)

            def split(hd):
                eng.wait_ge(hg_norm, hd + 1)
                eng.activation(chunk(mix_hi, 4 + hd), up[:, :], ACT.Copy).then_inc(mix_hi_ready, 1)

            for hd in range(4):
                eng.wait_ge(hg_o, hd + 1)
                if hd:
                    eng.wait_ge(hg_ms, hd)
                eng.activation(osq[:, :], bank(5 + hd % 2), ACT.Square).then_inc(hg_osq, 1)
                if hd:
                    split(hd - 1)
                eng.wait_ge(hg_ms, hd + 1)
                eng.activation((gated[:, :], chunk(sq, 1))[hd % 2], bank(7), ACT.Sqrt, bias=lbs[:, 31:32]).then_inc(hg_std, 1)
            split(3)

        def hgrn_dve(eng, link):
            l0 = COL["hgrn_lb_logits_2"]
            lb0, lb1 = vec[:, l0:l0 + 4], vec[:, l0 + 4:l0 + 8]
            link(eng.tensor_tensor(lb_s[:, 0:4], lb0, lb1, ALU.max))
            eng.tensor_tensor(lb_m[:, 0:4], lb0, lb_s[:, 0:4], ALU.subtract)
            eng.tensor_tensor(lb_m[:, 4:8], lb1, lb_s[:, 0:4], ALU.subtract).then_inc(lb_ready, 1)
            link(eng.memset(reset[:, :], 1.0))
            link(eng.memset(reset[:, 0:T:HGRN_BLOCK], 0.0))
            eng.wait_ge(hg_lb, 1)
            link(eng.tensor_tensor(lb_s[:, 0:4], lb_e[:, 0:4], lb_e[:, 4:8], ALU.add))
            link(eng.reciprocal(lb_s[:, 4:8], lb_s[:, 0:4]))
            link(eng.tensor_tensor(lb[:, 0:4], lb_e[:, 0:4], lb_s[:, 4:8], ALU.mult))
            link(eng.tensor_scalar(lb_rest[:, 0:4], lb[:, 0:4], -1.0, 1.0, ALU.mult, ALU.add))
            eng.wait_ge(hg_sig, 1)
            for hd in range(4):
                ins = eng.tensor_scalar(chunk(hf, hd), chunk(hk, hd), lb_rest[:, hd:hd + 1], lb[:, hd:hd + 1], ALU.mult, ALU.add)
            ins.then_inc(hg_f, 1)
            eng.wait_ge(hg_f, 1)
            eng.tensor_scalar(hk[:, :], hf, -1.0, 1.0, ALU.mult, ALU.add).then_inc(hg_f, 1)
            eng.memset(s_t[:, :], 0.0)
            eng.wait_ge(hg_ln, 1)
            for hd in range(4):
                ins = eng.tensor_tensor_scan(chunk(hc, hd), reset[:, :], chunk(hf, hd), 0.0, ALU.mult, ALU.add)
            ins.then_inc(hg_cum, 1)
            eng.wait_ge(hg_cum, 1)
            cum = hc[:, :].rearrange("p (b l) -> p b l", l=HGRN_BLOCK)
            eng.tensor_tensor(hf.rearrange("p (b l) -> p b l", l=HGRN_BLOCK),
                              cum[:, :, HGRN_BLOCK - 1:HGRN_BLOCK].to_broadcast([P, 4 * NHB, HGRN_BLOCK]), cum,
                              ALU.subtract).then_inc(hg_diff, 1)
            eng.wait_ge(hg_exp, 1)
            eng.tensor_tensor(hq, hq, he[:, :], ALU.mult).then_inc(hg_q, 1)
            eng.tensor_copy(decay, he[:, HGRN_BLOCK - 1::HGRN_BLOCK]).then_inc(hg_q, 1)
            eng.wait_ge(hg_exp, 2)
            eng.tensor_tensor(hkd[:, :], hk[:, :], hkd[:, :], ALU.mult).then_inc(hg_q, 1)
            eng.wait_ge(hg_exp, 3)
            eng.tensor_tensor(hc[:, :], hk[:, :], hf, ALU.mult).then_inc(hg_kend, 1)
            eng.wait_ge(hg_kend, 1)
            for hd in range(4):
                eng.wait_ge(hg_tp, 5 + hd)
                eng.tensor_copy(chunk(hk, hd), bank(4 + hd)).then_inc(hg_tb, 1)
            causal = mask[:, 2 * P:3 * P].bitcast(U32)

            def normed(hd):
                eng.wait_ge(hg_std, hd + 1)
                link(eng.reciprocal(gate[:, :], (gated[:, :], chunk(sq, 1))[hd % 2]))
                link(eng.scalar_tensor_tensor(prod[:, :], bank(5 + hd % 2), column(vec, COL["hgrn_norm_w_2"] + hd), gate[:, :],
                                              ALU.mult, ALU.mult))
                eng.wait_ge(hg_sig, 2)
                eng.wait_ge(mix_ready, KD + 4 + hd)
                eng.tensor_tensor(up[:, :], prod[:, :], chunk(hg, hd), ALU.mult).then_inc(hg_norm, 1)
                eng.wait_ge(mix_hi_ready, KD + 4 + hd + 1)
                eng.tensor_tensor(chunk(mix_lo, 4 + hd), up[:, :], chunk(mix_hi, 4 + hd).bitcast(F32), ALU.subtract)\
                    .then_inc(mix_ready, 1)

            for hd in range(4):
                eng.wait_ge(hg_s_ps, hd + 1)
                st4 = chunk(s_t, hd % 2).rearrange("p (n l) -> p n l", l=P)
                eng.copy_predicated(st4, causal[:, None, :].to_broadcast([P, NB, P]), bank(0).rearrange("p (n l) -> p n l", l=P))\
                    .then_inc(hg_s, 1)
                eng.wait_ge(hg_u_ps, hd + 1)
                if hd >= 2:
                    eng.wait_ge(hg_o, hd - 1)
                for b in range(NHB - 1):
                    grp, r = divmod(b, 4)
                    add = bank(1 + r)[:, grp * P:(grp + 1) * P]
                    to = state[hd % 2][:, state_col(b + 1)]
                    if b == 0:
                        eng.tensor_copy(to, add).then_inc(hg_state, 1)
                    else:
                        eng.wait_ge(hg_state, (NHB - 1) * hd + b)
                        eng.scalar_tensor_tensor(to, state[hd % 2][:, state_col(b)], decay[:, NHB * hd + b:NHB * hd + b + 1], add,
                                                 ALU.mult, ALU.add).then_inc(hg_state, 1)
                if hd:
                    normed(hd - 1)
            normed(3)

        block = ctx.enter_context(nc.Block())

        def wait_act(eng, sem, count):
            if not isinstance(count, int):
                count = eng.to_reg(count)
                eng.wait_ge(vec_landed, 32)
            wait(eng, sem, count)

        @block.sync
        def _(sp):
            sp.dma_start(vec[:, :], vecs).then_inc(vec_landed, 16)
            sp.dma_start(small[:, :], small_consts).then_inc(vec_landed, 16)
            sp.dma_start(h[:, :], x_t).then_inc(x_landed, 16)

            for st in stages:
                src = weights[st.name]

                def load(i, s, st=st, src=src):
                    per = 2 if st.kind == "in" else 4
                    slot = (st.q0 + s) % 2
                    wait(sp, lo_rounded, st.q0 + s - 1 + per * i)
                    if st.kind == "in":
                        n = PAIR
                        a = src[i * 2 + s] if isinstance(i, int) else src[bass.ds(i * 2 + s, 1)].rearrange("a p w -> (a p) w")
                    else:
                        m = i * 2 + s // 2
                        c0, n = ((0, 12 * P), (12 * P, 10 * P))[s % 2]
                        a = src[m] if isinstance(i, int) else src[bass.ds(m, 1)].rearrange("a p w -> (a p) w")
                        a = a[:, c0:c0 + n]
                    sp.dma_start(raw[:, slot * PAIR:slot * PAIR + n], a).then_inc(raw_landed[slot], 16)

                if st.kind == "in":
                    def body(i, load=load, u=2):
                        for s in range(u):
                            load(i, s)
                    repeat(sp, st.pairs // 2, body, first=1 if st.q0 == 0 else 0)
                    if st.pairs % 2:
                        body(st.pairs // 2, u=1)
                else:
                    def body(i, load=load):
                        for s in range(4):
                            load(i, s)
                    repeat(sp, KD // 2, body)

        @block.tensor
        def _(pe):
            def norm_matmul(r):
                pe.wait_ge(vec_landed, 32)
                pe.wait_ge(ssum_ready, KD * (r + 1))
                pe.matmul(bank(STATS_BANK), mean_d, ssum[:, :], start=True, stop=True).then_inc(ms_ready, 1)

            def product(b, hi, lo, rhs_hi, rhs_lo, start, stop):
                pe.matmul(bank(b), hi, rhs_hi, start=start, stop=False)
                pe.matmul(bank(b), hi, rhs_lo, start=False, stop=False)
                return pe.matmul(bank(b), lo, rhs_hi, start=False, stop=stop)

            def tile_of(w, slot, t):
                return w[:, slot * PAIR + t * P:slot * PAIR + (t + 1) * P]

            for st in stages:
                if st.name == "out1":
                    attention_pe(pe, 0)
                if st.name == "out2":
                    attention_pe(pe, 1)
                    hgrn_pe(pe)
                if st.name == "out3":
                    attention_pe(pe, 2)
                if st.kind == "in":
                    mixed = st.evac in ("add", "hold")
                    r_hi, r_lo = (mix_hi, mix_lo) if mixed else (x_split[:, 0:KD * T], x_split[:, KD * T:])
                    ready = (mix_ready, KD * ("out1", "out2", "out3").index(st.name)) if mixed else (x_ready, KD * st.x_index)

                    def body(i, u=2, st=st, r_hi=r_hi, r_lo=r_lo, ready=ready, mixed=mixed):
                        for s in range(u):
                            slot, pair_bank = (st.q0 + s) % 2, (st.g0 + s) % 2
                            wait(pe, lo_rounded, st.q0 + s + 1 + 2 * i)
                            wait(pe, evacuated, st.g0 + s - 1 + 2 * i)
                            for k in range(KD):
                                if s == 0:
                                    wait(pe, ready[0], ready[1] + k + 1)
                                for t in range(2):
                                    last = product(2 * pair_bank + t, tile_of(w_hi, slot, t * KD + k),
                                                   tile_of(w_lo, slot, t * KD + k), chunk(r_hi, k), chunk(r_lo, k),
                                                   k == 0, k == KD - 1)
                            last.then_inc(pair_done, 1)
                            if s == 0 and isinstance(i, int) and i == 0 and not mixed:
                                norm_matmul(st.stat)
                    repeat(pe, st.pairs // 2, body, first=1)
                    if st.pairs % 2:
                        body(st.pairs // 2, u=1)
                else:
                    a0 = KF * ("down1", "down2", "down3", "down4").index(st.name)

                    def body(i, st=st, a0=a0):
                        for mm in range(2):
                            b = 2 * ((st.g0 + mm) % 2)
                            wait(pe, evacuated, st.g0 + mm - 1 + 2 * i)
                            f = 0
                            for half in range(2):
                                s = 2 * mm + half
                                slot = (st.q0 + s) % 2
                                wait(pe, lo_rounded, st.q0 + s + 1 + 4 * i)
                                if mm == 0:
                                    wait(pe, act_ready, a0 + sum(HALF_TILES[:half + 1]))
                                for t in range(HALF_TILES[half]):
                                    last = product(b, tile_of(w_hi, slot, t), tile_of(w_lo, slot, t),
                                                   chunk(act, f), chunk(act, KF + f), f == 0, f == KF - 1)
                                    f += 1
                                last.then_inc(pair_done, 1)
                    repeat(pe, KD // 2, body)
                if st.name in BARRIERS:
                    norm_matmul(st.stat)

        def round_weights(eng, q, i, per):
            slot = q % 2
            wait(eng, raw_landed[slot], 16 * (q // 2 + 1) + 8 * per * i)
            wait(eng, pair_done, q - 1 + per * i)
            n = PAIR_TILES[q] * P
            w = slice(slot * PAIR, slot * PAIR + n)
            eng.activation(w_hi[:, w], raw[:, w], ACT.Copy).then_inc(hi_rounded, 1)

        def rest_weights(eng, q, i, per):
            slot = q % 2
            wait(eng, hi_rounded, q + 1 + per * i)
            n = PAIR_TILES[q] * P
            w = slice(slot * PAIR, slot * PAIR + n)
            eng.tensor_tensor(w_lo[:, w], raw[:, w], w_hi[:, w].bitcast(F32), ALU.subtract).then_inc(lo_rounded, 1)

        def square(eng, r, m, src, parity):
            wait_act(eng, ssum_ready, KD * r + m - 1)
            eng.activation(chunk(sq, parity), src, ACT.Square).then_inc(sq_ready, 1)

        def add_square(eng, r, m, parity):
            wait(eng, sq_ready, KD * r + m + 1)
            wait(eng, ssum_ready, KD * r + m)
            eng.tensor_tensor(ssum[:, :], ssum[:, :], chunk(sq, parity), ALU.add).then_inc(ssum_ready, 1)

        def round_x(eng, n, m, col):
            eng.activation(chunk(x_split, m), chunk(h, m), ACT.Copy, scale=column(vec, col + m)).then_inc(x_hi_ready, 1)

        def rest_x(eng, n, m, col):
            wait(eng, x_hi_ready, KD * n + m + 1)
            eng.scalar_tensor_tensor(chunk(x_split, KD + m), chunk(h, m), column(vec, col + m),
                                     chunk(x_split, m).bitcast(F32), ALU.mult, ALU.subtract).then_inc(x_ready, 1)

        @block.scalar
        def _(eng):
            def root(r):
                wait(eng, ms_ready, r + 1)
                eng.activation(chunk(std, 0), bank(STATS_BANK), ACT.Sqrt, bias=lbs[:, 31:32]).then_inc(std_ready, 1)

            eng.wait_ge(vec_landed, 32)
            eng.wait_ge(x_landed, 16)
            for m in range(KD):
                round_x(eng, 0, m, COL["ffn1_norm"])
                square(eng, 0, m, chunk(h, m), m % 2)
                if m == 1:
                    round_weights(eng, 0, 0, 0)
                if m == 5:
                    round_weights(eng, 1, 0, 0)

            for st in stages:
                if st.name == "out1":
                    attention_act(eng, 0)
                if st.name == "out2":
                    attention_act(eng, 1)
                    hgrn_act(eng)
                if st.name == "out3":
                    attention_act(eng, 2)
                if st.kind == "in" and st.evac in ("silu", "conv", "project"):
                    root(st.stat)
                f0 = KF * ("up1", "up2", "up3", "up4").index(st.name) if st.name.startswith("up") else 0

                def pair_step(i, s, per, st=st, f0=f0):
                    f = s + 2 * i
                    if st.evac in ("silu", "conv"):
                        wait(eng, gate_ready, f0 + 1 + f)
                        eng.activation(gated[:, :], gate[:, :], ACT.Silu if st.evac == "silu" else ACT.Gelu)\
                            .then_inc(gated_ready, 1)
                    if st.evac in ("add", "hold"):
                        if st.kind == "in":
                            ms, g = [2 * s + 4 * i, 2 * s + 1 + 4 * i], st.g0 + s + 2 * i
                        else:
                            ms, g = ([s // 2 + 2 * i], st.g0 + s // 2 + 2 * i) if s % 2 else ([], 0)
                        for k, m in enumerate(ms):
                            if k == 0:
                                wait_act(eng, evacuated, g + 1)
                            parity = k if st.kind == "in" else s // 2
                            if st.x_index is not None:
                                round_x(eng, st.x_index, m, st.next_norm)
                            square(eng, st.stat, m, chunk(h if st.evac == "add" else y, m), parity)
                    if isinstance(i, int) and st.q0 + s + per * i + 2 >= last_pair:
                        pass
                    elif isinstance(i, int):
                        round_weights(eng, st.q0 + s + per * i + 2, 0, 0)
                    else:
                        round_weights(eng, st.q0 + s + 2, i, per)
                    if st.evac in ("silu", "conv"):
                        wait_act(eng, prod_ready, f0 + 1 + f)
                        eng.activation(chunk(act, f), prod[:, :], ACT.Copy).then_inc(prod_hi, 1)

                if st.kind == "in":
                    def body(i, u=2):
                        for s in range(u):
                            pair_step(i, s, 2)
                    repeat(eng, st.pairs // 2, body, last=1)
                    if st.pairs % 2:
                        body(st.pairs // 2, u=1)
                else:
                    def body(i):
                        for s in range(4):
                            pair_step(i, s, 4)
                    repeat(eng, KD // 2, body, last=1)

                if st.name in BARRIERS:
                    bar = BARRIERS[st.name]
                    root(st.stat)
                    for m in range(KD if bar["x_index"] is not None else 0):
                        wait(eng, h_ready, bar["h0"] + m + 1)
                        round_x(eng, bar["x_index"], m, bar["next_col"])
                        square(eng, bar["stat"], m, chunk(h, m), m % 2)

        @block.vector
        def _(eng):
            steps = [0]

            def link(ins):
                steps[0] += 1
                ins.then_inc(dve_step, 1)
                eng.wait_ge(dve_step, steps[0])

            def inverse(r):
                wait(eng, std_ready, r + 1)
                eng.reciprocal(rstd[:, :], chunk(std, 0)).then_inc(rstd_ready, 1)
                wait(eng, rstd_ready, r + 1)

            eng.memset(lbs[:, :], EPS)
            link(eng.memset(shifted[:, 0:2], 0.0))
            link(eng.memset(ssum[:, :], 0.0))
            for m in range(KD):
                rest_x(eng, 0, m, COL["ffn1_norm"])
                add_square(eng, 0, m, m % 2)
                if m == 2:
                    rest_weights(eng, 0, 0, 0)
                if m == 6:
                    rest_weights(eng, 1, 0, 0)

            for st in stages:
                if st.name == "out1":
                    attention_dve(eng, 0, link)
                if st.name == "out2":
                    attention_dve(eng, 1, link)
                    hgrn_dve(eng, link)
                if st.name == "out3":
                    attention_dve(eng, 2, link)
                if st.kind == "in" and st.evac in ("silu", "conv", "project"):
                    inverse(st.stat)
                if st.evac in ("add", "hold"):
                    link(eng.memset(ssum[:, :], 0.0))
                f0 = KF * ("up1", "up2", "up3", "up4").index(st.name) if st.name.startswith("up") else 0
                conv0 = KF * (st.name == "up4")
                layer = int(st.name == "up4")

                def pair_step(i, s, per, st=st, f0=f0, conv0=conv0, layer=layer):
                    f = s + 2 * i
                    b = 2 * ((st.g0 + s) % 2) if st.kind == "in" else 2 * ((st.g0 + s // 2) % 2)
                    done = st.q0 + s + 1 + per * i
                    if st.evac in ("silu", "conv"):
                        wait(eng, pair_done, done)
                        if st.evac == "silu":
                            eng.tensor_tensor(gate[:, :], bank(b), rstd[:, :], ALU.mult).then_inc(gate_ready, 1)
                            eng.tensor_tensor(up[:, :], bank(b + 1), rstd[:, :], ALU.mult).then_inc(evacuated, 1)
                        else:
                            eng.tensor_tensor(shifted[:, 2:], bank(b), rstd[:, :], ALU.mult).then_inc(u_ready, 1)
                            eng.tensor_tensor(up[:, :], bank(b + 1), rstd[:, :], ALU.mult).then_inc(evacuated, 1)
                            cw = COL["ffn_conv_w_2"] + layer * 3 * KF
                            tap = [column(vec, cw + j * KF + f) for j in range(3)]
                            cb = column(vec, COL["ffn_conv_b_2"] + layer * KF + f)
                            wait(eng, u_ready, conv0 + 1 + f)
                            eng.tensor_scalar(prod[:, :], shifted[:, 2:], tap[2], cb, ALU.mult, ALU.add)\
                                .then_inc(conv_a, 1)
                            wait(eng, conv_a, conv0 + 1 + f)
                            eng.scalar_tensor_tensor(gate[:, :], shifted[:, 1:T + 1], tap[1], prod[:, :], ALU.mult, ALU.add)\
                                .then_inc(conv_b, 1)
                            wait(eng, conv_b, conv0 + 1 + f)
                            eng.scalar_tensor_tensor(gate[:, :], shifted[:, 0:T], tap[0], gate[:, :], ALU.mult, ALU.add)\
                                .then_inc(gate_ready, 1)
                        wait(eng, gated_ready, f0 + 1 + f)
                        wait(eng, evacuated, st.g0 + s + 1 + 2 * i)
                        eng.tensor_tensor(prod[:, :], gated[:, :], up[:, :], ALU.mult).then_inc(prod_ready, 1)
                    elif st.evac == "project":
                        wait(eng, pair_done, done)
                        out = chunk(proj, f, 2 * T).rearrange("p (a t) -> p a t", a=2)
                        both = bank(b, 2).rearrange("p (a t) -> p a t", a=2)
                        eng.tensor_tensor(out, both, rstd[:, None, :].to_broadcast([P, 2, T]), ALU.mult)\
                            .then_inc(evacuated, 1)
                    elif st.kind == "in" or s % 2:
                        wait_act(eng, pair_done, done)
                        ms = [2 * s + 4 * i, 2 * s + 1 + 4 * i] if st.kind == "in" else [s // 2 + 2 * i]
                        for k, m in enumerate(ms):
                            if st.evac == "add":
                                ins = eng.scalar_tensor_tensor(chunk(h, m), bank(b + k), st.factor, chunk(h, m), ALU.mult, ALU.add)
                            else:
                                ins = eng.tensor_copy(chunk(y, m), bank(b + k))
                        ins.then_inc(evacuated, 1)
                        for k, m in enumerate(ms):
                            if st.x_index is not None:
                                rest_x(eng, st.x_index, m, st.next_norm)
                            add_square(eng, st.stat, m, k if st.kind == "in" else s // 2)
                    if isinstance(i, int) and st.q0 + s + per * i + 2 >= last_pair:
                        pass
                    elif isinstance(i, int):
                        rest_weights(eng, st.q0 + s + per * i + 2, 0, 0)
                    else:
                        rest_weights(eng, st.q0 + s + 2, i, per)
                    if st.evac in ("silu", "conv"):
                        wait(eng, prod_hi, f0 + 1 + f)
                        eng.tensor_tensor(chunk(act, KF + f), prod[:, :], chunk(act, f).bitcast(F32), ALU.subtract)\
                            .then_inc(act_ready, 1)

                if st.kind == "in":
                    def body(i, u=2):
                        for s in range(u):
                            pair_step(i, s, 2)
                    repeat(eng, st.pairs // 2, body, last=1)
                    if st.pairs % 2:
                        body(st.pairs // 2, u=1)
                else:
                    def body(i):
                        for s in range(4):
                            pair_step(i, s, 4)
                    repeat(eng, KD // 2, body, last=1)

                if st.name in BARRIERS:
                    bar = BARRIERS[st.name]
                    inverse(st.stat)
                    if bar["x_index"] is not None:
                        link(eng.memset(ssum[:, :], 0.0))
                    scaled = [gate, gated]
                    b0 = bar["h0"] - 8
                    for m in range(KD + 1):
                        if m < KD:
                            if bar["kind"] == "final":
                                eng.scalar_tensor_tensor(chunk(h, m), chunk(h, m), column(vec, bar["col"] + m), rstd[:, :],
                                                         ALU.mult, ALU.mult).then_inc(h_ready, 1)
                            else:
                                wait(eng, h_ready, bar["h0"] + m - 1)
                                eng.scalar_tensor_tensor(scaled[m % 2][:, :], chunk(y, m), column(vec, bar["col"] + m),
                                                         rstd[:, :], ALU.mult, ALU.mult).then_inc(scaled_ready, 1)
                        if m >= 1 and bar["x_index"] is not None:
                            rest_x(eng, bar["x_index"], m - 1, bar["next_col"])
                            add_square(eng, bar["stat"], m - 1, (m - 1) % 2)

        @block.gpsimd
        def _(eng):
            eng.dma_start(sink_col, sinks.to_broadcast([P, 16])).then_inc(sink_landed, 16)
            eng.dma_start(scratch[:, 3 * P:5 * P], rel_bias[:, 1:257]).then_inc(table_landed, 16)
            eng.dma_start(tiny[0:16, 240:242], rel_bias[:, 0:2]).then_inc(table_landed, 16)
            eng.wait_ge(table_landed, 32)
            eng.tensor_copy(shifted[0:16, 2:2 + 3 * P], tiny[0:16, 240:241].to_broadcast([16, 3 * P])).then_inc(far_ready, 1)
            eng.wait_ge(far_ready, 1)
            eng.dma_start(scratch[:, 0:3 * P], shifted[0:16, 2:2 + 3 * P]).then_inc(table_landed, 16)
            eng.wait_ge(table_landed, 48)
            eng.dma_start(skew.rearrange("h (p w) -> h p w", w=5 * P + 1)[:, :, 0:5 * P],
                          scratch[:, None, :].to_broadcast([16, P, 5 * P])).then_inc(table_landed, 16)

            for st in stages:
                if st.evac == "project":
                    eng.wait_ge(pair_done, st.q0)
                    a = ("in1", "in2", "in3").index(st.name)
                    eng.dma_start(mconst[:, :], mixer_consts[a]).then_inc(const_landed, 16)
                    if a == 0:
                        eng.dma_start(ptab[:, :], pool_tab).then_inc(tab_landed, 16)
                        eng.dma_start(pw[:, :], pool_w).then_inc(tab_landed, 16)
                if st.name == "out1":
                    pool_gpsimd(eng)
                if st.name == "out3":
                    bias_gpsimd(eng)
                if st.name in BARRIERS and BARRIERS[st.name]["kind"] == "post":
                    bar = BARRIERS[st.name]
                    for m in range(KD):
                        wait(eng, scaled_ready, bar["h0"] - 8 + m + 1)
                        eng.tensor_tensor(chunk(h, m), chunk(h, m), (gate, gated)[m % 2][:, :], ALU.add).then_inc(h_ready, 1)
            if stop is not None:
                eng.wait_ge(evacuated, stages[-1].g0 + stages[-1].groups)
                if stages[-1].name in BARRIERS:
                    eng.wait_ge(h_ready, BARRIERS[stages[-1].name]["h0"] + KD)
                eng.dma_start(out_t, h[:, :]).then_inc(out_landed, 16)
                eng.wait_ge(out_landed, 16)
            else:
                for m in range(KD):
                    eng.wait_ge(h_ready, BARRIERS["down4"]["h0"] + m + 1)
                    eng.dma_start(out_t[:, m * T:(m + 1) * T], chunk(h, m)).then_inc(out_landed, 16)
                eng.wait_ge(out_landed, 16 * KD)


def lay_out(inputs):
    a = {k: np.asarray(v) for k, v in inputs.items()}
    feat = lambda v: v.reshape(-1, P).T
    x_t = a["x"][0].T.reshape(KD, P, T).transpose(1, 0, 2).reshape(P, KD * T)
    vecs = np.concatenate([feat(a[n].reshape(-1)) for n, _ in _VECS], axis=1)

    def tiles(w):
        k, m = w.shape
        return w.reshape(k // P, P, m // P, P).transpose(2, 1, 0, 3).reshape(m // P, P, k)

    def pairs(t):
        return t.reshape(-1, 2, P, t.shape[-1]).transpose(0, 2, 1, 3).reshape(-1, P, 2 * t.shape[-1])

    def twin(g, u):
        return pairs(np.stack([tiles(g), tiles(u)], axis=1).reshape(2 * KF, P, D))

    w = {}
    w["up1"] = twin(a["ffn1_w_gate"][0], a["ffn1_w_up"][0])
    w["down1"] = tiles(a["ffn1_w_down"][0])
    w["in1"] = pairs(tiles(a["w_in"][0]))
    w["out1"] = pairs(tiles(a["w_out"][0]))
    w["up2"] = twin(a["ffn2_w_gate"][0], a["ffn2_w_up"][0])
    w["down2"] = tiles(a["ffn2_w_down"][0])
    w["in2"] = pairs(tiles(a["even_w_in_2"][0]))
    w["out2"] = pairs(tiles(a["even_w_out_2"][0]))
    w["up3"] = twin(a["ffn_w_up_2"][0][:, :F], a["ffn_w_up_2"][0][:, F:])
    w["down3"] = tiles(a["ffn_w_down_2"][0])
    w["in3"] = pairs(tiles(a["odd_w_in_2"][0]))
    w["out3"] = pairs(tiles(a["odd_w_out_2"][0]))
    w["up4"] = twin(a["ffn_w_up_2"][1][:, :F], a["ffn_w_up_2"][1][:, F:])
    w["down4"] = tiles(a["ffn_w_down_2"][1])
    arrays = {"x_t": x_t, "vecs": vecs, **{f"w_{n}": v for n, v in w.items()}}
    arrays["pool_w"] = a["pool_w"][0].transpose(1, 0, 2).reshape(P, 4 * P)
    arrays["sinks"] = np.concatenate([a["sink_logits"][0], a["even_sinks_2"][0]]).reshape(1, 16)
    arrays["rel_bias"] = a["odd_rel_bias_2"][0][:, ::-1]
    return arrays


def shape_constants():
    t = np.arange(T, dtype=np.float32)
    p = np.arange(P)
    eye = np.eye(P, dtype=np.float32)

    def rotary(theta, dim, head=64):
        half = dim // 2
        inv = (np.float32(theta) ** (-np.arange(0, dim, 2, dtype=np.float32) / np.float32(dim))).astype(np.float32)
        c, s, pm = np.ones((P, T), np.float32), np.zeros((P, T), np.float32), np.zeros((P, P), np.float32)
        for m in range(P):
            d = m % head
            if d < dim:
                ang = t * inv[d % half]
                c[m], s[m] = np.cos(ang), np.sin(ang)
                if d < half:
                    pm[m + half, m] = -1.0
                else:
                    pm[m - half, m] = 1.0
        return c, s, pm

    def picks(pm):
        sel = [np.zeros((P, P), np.float32) for _ in range(2)]
        for g in range(2):
            for m in range(P):
                sel[g][64 * g + m % 64, m] = 1.0
        return sel, [(s @ pm).astype(np.float32) for s in sel]

    q, k = p[:, None], np.arange(384)[None, :]
    neg = np.float32(-8 * BIG)
    m0 = np.where(np.abs(q + P - k) <= P, 0, neg)
    chunk_q, chunk_k = 2 + q // 64, np.arange(384)[None, :] // 64
    m1 = np.where((chunk_k <= chunk_q) & (chunk_k >= chunk_q - 2), 0, neg)
    m1[:, 256:384] = 0
    same = (p[:, None] // HGRN_BLOCK == p[None, :] // HGRN_BLOCK) & (p[:, None] <= p[None, :])
    m1[:, 256:384] = same
    m2 = np.zeros((P, 384))
    m2[:, 0:P] = np.where(p[None, :] // 64 <= p[:, None] // 64, 0, neg)
    mixers = []
    for (theta, dim), mk in (((500000.0, 16), m0), ((10000.0, 64), m1), ((10000.0, 64), m2)):
        c, s, pm = rotary(theta, dim)
        sel, selp = picks(pm)
        mixers.append(np.concatenate([c, s, mk.astype(np.float32), pm, *sel, *selp], axis=1))
    tab = np.zeros((4, TAIL), np.float32)
    for g, w in enumerate(POOL_WINDOWS):
        tt = np.arange(T + 1)
        n = np.minimum(tt + w // 2, T) - np.maximum(tt - w // 2, 0)
        tab[g, :T + 1] = 0.5 / n
    tab = np.broadcast_to(tab.reshape(1, -1), (P, 4 * TAIL))
    small = np.concatenate([eye, np.full((P, P), 1.0 / D, np.float32), np.full((P, P), 1.0 / P, np.float32)], axis=1)
    return {"mixer_consts": np.stack(mixers), "pool_tab": tab, "small_consts": small}


def kernel(**inputs):
    import concourse.bacc as bacc
    from concourse.bass_utils import run_bass_kernel_spmd as run

    nc = bacc.Bacc("TRN2", target_bir_lowering=False, num_devices=1)
    arrays = {**lay_out(inputs), **shape_constants()}
    arrays = {n: np.ascontiguousarray(v, dtype=None) for n, v in arrays.items()}
    ap = {n: nc.dram_tensor(f"in_{n}", v.shape, F32, kind="ExternalInput").ap() for n, v in arrays.items()}
    out_t = nc.dram_tensor("out_t", (P, KD * T), F32, kind="ExternalOutput").ap()
    scratch = nc.dram_tensor("scratch", (16, 5 * P), F32).ap()
    skew = nc.dram_tensor("skew", (16, P * (5 * P + 1)), F32).ap()
    build(nc, ap["x_t"], ap["vecs"], {s.name: ap[f"w_{s.name}"] for s in STAGES}, ap["mixer_consts"], ap["pool_tab"],
          ap["small_consts"], ap["pool_w"], ap["sinks"], ap["rel_bias"], out_t, scratch, skew, stop=STOP)
    r = run(nc, [{f"in_{n}": v for n, v in arrays.items()}], core_ids=[0])
    o = r.results[0]["out_t"]
    return o.reshape(P, KD, T).transpose(2, 1, 0).reshape(1, T, D)


STOP = None
```

```python
import concourse.bass as bass
import numpy as np
from concourse import mybir
from contextlib import ExitStack

F32 = mybir.dt.float32
F32R = mybir.dt.float32r
U32 = mybir.dt.uint32
ALU = mybir.AluOpType
ACT = mybir.ActivationFunctionType

P = 128
T = 512
D = 1024
KD = D // P
F = 2816
KF = F // P
NB = T // P
EPS = 1e-6
BIG = 1e30
HALF_TILES = (12, 10)
PAIR = 2 * KD * P
X_LOADS = 4
HGRN_BLOCK = 32
NHB = T // HGRN_BLOCK
POOL_WINDOWS = (2, 4, 8, 16)
PAD = 8
TAIL = 516

_VECS = [
    ("ffn1_norm", KD), ("mix_norm", KD), ("ffn2_norm", KD), ("final_norm", KD), ("norm_w_2", 8 * KD),
    ("ffn_conv_w_2", 2 * 3 * KF), ("ffn_conv_b_2", 2 * KF), ("pool_scale", 4), ("hgrn_norm_w_2", 4),
    ("hgrn_lb_logits_2", 8),
]
COL = {}
_c = 0
for _name, _n in _VECS:
    COL[_name] = _c
    _c += _n
NVEC = _c



class Stage:
    def __init__(self, name, kind, pairs, groups, evac):
        self.name, self.kind, self.pairs, self.groups, self.evac = name, kind, pairs, groups, evac


STAGES = [
    Stage("up1", "in", KF, KF, "silu"), Stage("down1", "down", 2 * KD, KD, "add"),
    Stage("in1", "in", 5, 5, "project"), Stage("out1", "in", KD // 2, KD // 2, "add"),
    Stage("up2", "in", KF, KF, "silu"), Stage("down2", "down", 2 * KD, KD, "add"),
    Stage("in2", "in", 11, 11, "project"), Stage("out2", "in", KD // 2, KD // 2, "hold"),
    Stage("up3", "in", KF, KF, "conv"), Stage("down3", "down", 2 * KD, KD, "hold"),
    Stage("in3", "in", 12, 12, "project"), Stage("out3", "in", KD // 2, KD // 2, "hold"),
    Stage("up4", "in", KF, KF, "conv"), Stage("down4", "down", 2 * KD, KD, "hold"),
]
_q = _g = 0
PAIR_TILES = []
for _s in STAGES:
    _s.q0, _s.g0 = _q, _g
    _q += _s.pairs
    _g += _s.groups
    PAIR_TILES += [2 * KD] * _s.pairs if _s.kind == "in" else list(HALF_TILES) * KD
NPAIR = _q
BY = {s.name: s for s in STAGES}
for _n, _x, _r in (("up1", 0, 0), ("in1", 1, 1), ("up2", 2, 2), ("in2", 3, 4), ("up3", 4, 6), ("in3", 5, 8), ("up4", 6, 10)):
    BY[_n].x_index, BY[_n].stat = _x, _r
for _n, _x, _r, _v, _f in (("down1", 1, 1, "mix_norm", 0.5), ("out1", 2, 2, "ffn2_norm", 1.0), ("down2", None, 3, None, 0.5),
                           ("out2", None, 5, None, 1.0), ("down3", None, 7, None, 1.0), ("out3", None, 9, None, 1.0),
                           ("down4", None, 11, None, 1.0)):
    BY[_n].x_index, BY[_n].stat, BY[_n].next_norm, BY[_n].factor = _x, _r, (COL[_v] if _v else None), _f
NW = COL["norm_w_2"]
BARRIERS = {
    "down2": dict(kind="final", col=COL["final_norm"], next_col=NW + 0 * KD, x_index=3, stat=4, h0=0),
    "out2": dict(kind="post", col=NW + 1 * KD, next_col=NW + 2 * KD, x_index=4, stat=6, h0=8),
    "down3": dict(kind="post", col=NW + 3 * KD, next_col=NW + 4 * KD, x_index=5, stat=8, h0=16),
    "out3": dict(kind="post", col=NW + 5 * KD, next_col=NW + 6 * KD, x_index=6, stat=10, h0=24),
    "down4": dict(kind="post", col=NW + 7 * KD, next_col=None, x_index=None, stat=None, h0=32),
}
IN2_ORDER = [*range(10, 14), *range(6, 10), *range(18, 22), *range(14, 18), *range(0, 6)]
ATTENTIONS = [
    dict(heads=8, grouped=True, back=1, ahead=1, q=0, k=4, v=5),
    dict(heads=8, grouped=True, back=1, ahead=0, q=16, k=20, v=21),
    dict(heads=16, grouped=False, back=NB, ahead=0, q=0, k=8, v=16),
]
for _i, _a in enumerate(ATTENTIONS):
    _a["units"] = []
    for _h in range(_a["heads"]):
        for _n in range(NB):
            _lo, _hi = max(0, _n - _a["back"]), min(NB - 1, _n + _a["ahead"])
            _a["units"].append((_h // 2, _h % 2, _n, _lo, _hi - _lo + 1))
    _a["u0"] = sum(len(b["units"]) for b in ATTENTIONS[:_i])


def wait(eng, sem, count):
    if not isinstance(count, int) or count > 0:
        eng.wait_ge(sem, count)


def chunk(t, m, width=T):
    if isinstance(m, int):
        return t[:, m * width:(m + 1) * width]
    return t[:, bass.ds(m * width, width)]


def column(t, c):
    return t[:, c:c + 1] if isinstance(c, int) else t[:, bass.ds(c, 1)]


def repeat(eng, n, body, first=0, last=0):
    first = min(first, n)
    last = min(last, n - first)
    for i in range(first):
        body(i)
    middle = n - first - last
    if middle == 1:
        body(first)
    elif middle > 1:
        with eng.Fori(first, n - last) as i:
            body(i)
    for i in range(n - last, n):
        body(i)


def build(nc, x_t, vecs, weights, mixer_consts, pool_tab, small_consts, pool_w, sinks, rel_bias, out_t, scratch, skew, stop=None):
    names = [s.name for s in STAGES]
    stages = STAGES if stop is None else STAGES[:names.index(stop) + 1]
    last_pair = stages[-1].q0 + stages[-1].pairs

    with ExitStack() as ctx:
        base = nc.sbuf_base
        place = [(base + 31) // 32 * 32]
        SLOT = T * 4

        def at(name, shape, dt, offset):
            return nc.alloc_sbuf_tensor_at(name, shape, dt, offset=offset)

        def new(name, words, dt=F32):
            t = at(name, [P, words], dt, place[0])
            place[0] += (words * 4 + 31) // 32 * 32
            return t

        def sem(name):
            return ctx.enter_context(nc.semaphore(name))

        act_at = place[0]
        act = new("act", 2 * KF * T, F32R)
        x_at = place[0]
        x_split = new("x_split", 2 * KD * T, F32R)
        h = new("h", KD * T)
        raw = new("raw", 2 * PAIR)
        w_hi = new("w_hi", 2 * PAIR, F32R)
        w_lo = new("w_lo", 2 * PAIR, F32R)
        gate = new("gate", T)
        gated = new("gated", T)
        up = new("up", T)
        prod = new("prod", T)
        shifted = new("shifted", T + 2)
        sq = new("sq", 2 * T)
        ssum = new("ssum", T)
        rstd = new("rstd", T)
        vec = new("vec", NVEC)
        small = new("small", 3 * P)
        lbs = new("lbs", 32)
        tiny = new("tiny", 256)
        arena_words = (place[0] - base + 3) // 4
        ctx.enter_context(nc.sbuf_tensor("arena", [P, arena_words], F32))
        ident, mean_d, mean_head = small[:, 0:P], small[:, P:2 * P], small[:, 2 * P:3 * P]

        proj = at("proj", [P, 24 * T], F32, act_at)
        mconst = at("mconst", [P, 4 * T], F32, act_at + 24 * SLOT)
        mix_hi = act[:, 28 * T:36 * T]
        mix_lo = act[:, 36 * T:44 * T]
        cos, sin = mconst[:, 0:T], mconst[:, T:2 * T]
        mask = mconst[:, 2 * T:2 * T + 384]
        perm = mconst[:, 2 * T + 384:3 * T]
        pick = [mconst[:, 3 * T + g * P:3 * T + (g + 1) * P] for g in range(2)]
        pick_perm = [mconst[:, 3 * T + (2 + g) * P:3 * T + (3 + g) * P] for g in range(2)]
        squares = at("squares", [P, KD * T], F32, act_at)
        y = at("y", [P, KD * T], F32, x_at)
        xs = lambda n, words, k: at(n, [P, words], F32, x_at + k * SLOT)
        rot_a, rot_b = xs("rot_a", T, 0), xs("rot_b", T, 1)
        kdup = xs("kdup", 2 * T, 2)
        v_tok = xs("v_tok", 2 * T, 4)
        spare = [xs(f"spare{k}", T, k) for k in (0, 1, 14, 15)]
        near = [xs(f"near{k}", T, k) for k in range(6, 12)]
        score = [near[:2] + [spare[s]] for s in (2, 2, 0)]
        prob = [near[2:] + [spare[s]] for s in (3, 3, 1)]
        prob_t = xs("prob_t", 2 * T, 12)
        up_at = lambda n, words, k: at(n, [P, words], F32, act_at + k * SLOT)
        pw = up_at("pw", 4 * P, 11)
        pool_d = [up_at(f"pool_d{g}", T, k) for g, k in enumerate((10, 12, 13, 23))]
        ptab = up_at("ptab", 4 * TAIL, 14)
        csum = up_at("csum", T + 1 + 2 * PAD, 19)
        pool_e = up_at("pool_e", T + 1, 21)
        hf, hq, hg, hv = (proj[:, k * T:(k + 4) * T] for k in (0, 4, 8, 12))
        he, hk, hc = up_at("he", 4 * T, 28), up_at("hk", 4 * T, 32), up_at("hc", 4 * T, 40)
        state = [xs("state0", 4 * T, 8), xs("state1", 4 * T, 12)]
        s_t = up_at("s_t", 2 * T, 20)
        osq = up_at("osq", T, 22)
        biases = [up_at("bias0", T, 35), up_at("bias1", T, 43)]
        reset = up_at("reset", T, 23)

        ps = ctx.enter_context(nc.psum_tensor("ps", [P, 8 * T], F32))
        bank = lambda b, n=1: ps[:, b * T:(b + n) * T]
        STATS_BANK, WARM_BANK = 4, 7

        raw_landed = [sem(f"raw_landed{k}") for k in range(2)]
        x_landed = [sem(f"x_landed{k}") for k in range(X_LOADS)]
        vec_landed = sem("vec_landed")
        hi_rounded = sem("hi_rounded")
        lo_rounded = sem("lo_rounded")
        pair_done = sem("pair_done")
        evacuated = sem("evacuated")
        gate_ready = sem("gate_ready")
        gated_ready = sem("gated_ready")
        prod_ready = sem("prod_ready")
        prod_hi = sem("prod_hi")
        act_ready = sem("act_ready")
        u_ready = sem("u_ready")
        conv_a = sem("conv_a")
        conv_b = sem("conv_b")
        x_hi_ready = sem("x_hi_ready")
        x_ready = sem("x_ready")
        sq_ready = sem("sq_ready")
        ssum_ready = sem("ssum_ready")
        ms_ready = sem("ms_ready")
        std_ready = sem("std_ready")
        diag_ready = sem("diag_ready")
        spread = sem("spread")
        rstd_ready = sem("rstd_ready")
        h_ready = sem("h_ready")
        scaled_ready = sem("scaled_ready")
        mix_hi_ready = sem("mix_hi_ready")
        mix_ready = sem("mix_ready")
        out_landed = sem("out_landed")
        dve_step = sem("dve_step")
        pool_step = sem("pool_step")
        const_landed = sem("const_landed")
        tab_landed = sem("tab_landed")
        sink_landed = sem("sink_landed")
        rope_ps = sem("rope_ps")
        rope_done = sem("rope_done")
        kdup_done = sem("kdup_done")
        v_ps = sem("v_ps")
        v_done = sem("v_done")
        scores_ps = sem("scores_ps")
        neg_max = sem("neg_max")
        probs = sem("probs")
        probs_t_ps = sem("probs_t_ps")
        probs_normed = sem("probs_normed")
        probs_t = sem("probs_t")
        weighed = sem("weighed")
        far_ready = sem("far_ready")
        csum_done = sem("csum_done")
        csum_used = sem("csum_used")
        pool_diff = sem("pool_diff")
        pool_ps = sem("pool_ps")
        bias_landed = [sem(f"bias_landed{k}") for k in range(2)]
        bias_scaled = sem("bias_scaled")
        bias_ready = sem("bias_ready")
        table_landed = sem("table_landed")
        hg_sig = sem("hg_sig")
        hg_lb = sem("hg_lb")
        lb_ready = sem("lb_ready")
        hg_tb = sem("hg_tb")
        hg_f = sem("hg_f")
        hg_ln = sem("hg_ln")
        hg_cum = sem("hg_cum")
        hg_exp = sem("hg_exp")
        hg_diff = sem("hg_diff")
        hg_kend = sem("hg_kend")
        hg_q = sem("hg_q")
        hg_tp = sem("hg_tp")
        hg_ta = sem("hg_ta")
        hg_s_ps = sem("hg_s_ps")
        hg_s = sem("hg_s")
        hg_u_ps = sem("hg_u_ps")
        hg_state = sem("hg_state")
        hg_o = sem("hg_o")
        hg_osq = sem("hg_osq")
        hg_ms = sem("hg_ms")
        hg_std = sem("hg_std")
        hg_diag = sem("hg_diag")
        hg_spread = sem("hg_spread")
        hg_norm = sem("hg_norm")

        NEG, ROW, INV = (tiny[:, 16 * k:16 * (k + 1)] for k in range(3))
        std4, inv4 = tiny[:, 112:116], tiny[:, 116:120]
        sink_col, neg_sink, decay = tiny[:, 80:96], tiny[:, 96:112], tiny[:, 128:192]
        lb_m, lb_e, lb_s, lb, lb_rest = (tiny[:, 192 + 8 * k:200 + 8 * k] for k in range(5))
        IN = ("in1", "in2", "in3")
        LAG_N, LAG_T, LAG_V, LAG_MIX, AHEAD = 2, 4, 5, 6, (3, 3, 9)

        def projected(a):
            s = BY[IN[a]]
            return s.g0 + s.groups

        def stat_col(c, hh, n):
            k = 8 * (c % 2) + 4 * hh + n
            return slice(k, k + 1)

        def key_bias(a, c, hh, n, lo, nk):
            if a < 2:
                off = (lo - (n - 1)) * P
                return mask[:, off:off + nk * P]
            off = (NB - 1 - n) * P
            return biases[hh][:, off:off + nk * P]

        def attention_pe(pe, a):
            at_, units = ATTENTIONS[a], ATTENTIONS[a]["units"]
            u0, nc_ = at_["u0"], at_["heads"] // 2
            pe.wait_ge(evacuated, projected(a))
            pe.wait_ge(const_landed, 16 * (a + 1))

            def values(c):
                b = 3 if a < 2 else 7
                src = at_["v"] + (c if a == 2 else 0)
                for n in range(NB):
                    ins = pe.transpose(bank(b)[:, n * P:(n + 1) * P], proj[:, src * T + n * P:src * T + (n + 1) * P], ident)
                ins.then_inc(v_ps, 1)

            def rotate(c):
                pe.matmul(bank(7), perm, chunk(proj, at_["q"] + c), start=True, stop=True).then_inc(rope_ps, 1)

            if a < 2:
                for g in range(2):
                    pe.matmul(bank(7 - 2 * g), pick[g], chunk(proj, at_["k"]), start=True, stop=True)
                    pe.matmul(bank(6 - 2 * g), pick_perm[g], chunk(proj, at_["k"]), start=True, stop=True).then_inc(rope_ps, 1)
                values(0)
                pe.wait_ge(kdup_done, 2 * a + 1)
                rotate(0)
                pe.wait_ge(v_done, a + 1)
            else:
                values(0)
            for step in range(len(units) + LAG_MIX + 1):
                if step < len(units):
                    c, hh, n, lo, nk = units[step]
                    if hh == 0 and n == 0 and a < 2:
                        pe.wait_ge(rope_done, 4 * a + c + 1)
                        pe.wait_ge(kdup_done, 2 * a + 2)
                    if step >= 3:
                        pe.wait_ge(neg_max, u0 + step - 2)
                    rows = slice(64 * hh, 64 * hh + 64)
                    if a < 2:
                        k_ap = kdup[rows, (c // 2) * T + lo * P:(c // 2) * T + (lo + nk) * P]
                    else:
                        k_ap = proj[rows, (at_["k"] + c) * T + lo * P:(at_["k"] + c) * T + (lo + nk) * P]
                    qs = (at_["q"] + c) * T + n * P
                    pe.matmul(bank(step % 3)[:, 0:nk * P], proj[rows, qs:qs + P], k_ap, start=True, stop=True)\
                        .then_inc(scores_ps, 1)
                u = step - LAG_T
                if 0 <= u < len(units):
                    nk = units[u][4]
                    pe.wait_ge(probs_normed, u0 + u + 1)
                    if u >= 2:
                        pe.wait_ge(probs_t, u0 + u - 1)
                    for j in range(nk):
                        ins = pe.transpose(bank(3 + u % 2)[:, j * P:(j + 1) * P], prob[a][u % 5][:, j * P:(j + 1) * P], ident)
                    ins.then_inc(probs_t_ps, 1)
                u = step - LAG_V
                if 0 <= u < len(units):
                    c, hh, n, lo, nk = units[u]
                    if hh == 0 and n == 0:
                        if c >= 2:
                            pe.wait_ge(mix_ready, KD * a + c - 1)
                        if a == 2:
                            pe.wait_ge(v_done, 2 + c + 1)
                    pe.wait_ge(probs_t, u0 + u + 1)
                    for j in range(nk):
                        vc = (lo + j) * P + (64 * (c // 2) if a < 2 else (c % 2) * T + 64 * hh)
                        ins = pe.matmul(bank(5 + c % 2)[64 * hh:64 * hh + 64, n * P:(n + 1) * P], v_tok[:, vc:vc + 64],
                                        prob_t[:, (u % 2) * T + j * P:(u % 2) * T + (j + 1) * P], start=j == 0, stop=j == nk - 1)
                    ins.then_inc(weighed, 1)
                c, e = divmod(step - AHEAD[a], 8)
                if e == 0 and 0 <= c < nc_ - 1:
                    if a < 2:
                        rotate(c + 1)
                    else:
                        values(c + 1)
            if a == 0:
                pe.wait_ge(mix_ready, nc_)
                pe.wait_ge(tab_landed, 32)
                for g in range(4):
                    pe.wait_ge(pool_diff, g + 1)
                    pe.matmul(bank(4 + g), pw[:, g * P:(g + 1) * P], pool_d[g][:, :], start=True, stop=True).then_inc(pool_ps, 1)

        def attention_act(eng, a):
            at_, units = ATTENTIONS[a], ATTENTIONS[a]["units"]
            u0, nc_ = at_["u0"], at_["heads"] // 2

            def values(c):
                eng.wait_ge(v_ps, (a if a < 2 else 2 + c) + 1)
                if a == 2 and c >= 2:
                    eng.wait_ge(weighed, u0 + 8 * (c - 1))
                eng.activation(chunk(v_tok, c % 2 if a == 2 else 0), bank(7 if a == 2 else 3), ACT.Copy).then_inc(v_done, 1)

            values(0)
            for step in range(len(units) + LAG_MIX + 1):
                u = step - LAG_T
                if 0 <= u < len(units):
                    eng.wait_ge(probs_t_ps, u0 + u + 1)
                    if u >= 2:
                        eng.wait_ge(weighed, u0 + u - 1)
                    w = units[u][4] * P
                    eng.activation(prob_t[:, (u % 2) * T:(u % 2) * T + w], bank(3 + u % 2)[:, 0:w], ACT.Copy).then_inc(probs_t, 1)
                if step < len(units):
                    c, hh, n, lo, nk = units[step]
                    k = stat_col(c, hh, n)
                    w = nk * P + (a < 2)
                    eng.wait_ge(neg_max, u0 + step + 1)
                    if step >= 5:
                        eng.wait_ge(probs_t_ps, u0 + step - 4)
                    eng.activation(prob[a][step % 5][:, 0:w], score[a][step % 3][:, 0:w],
                                   ACT.Exp, bias=NEG[:, k], scale=-1.0, accum_out=ROW[:, k]).then_inc(probs, 1)
                c, e = divmod(step - 7 - LAG_MIX, 8)
                if e == 0 and 0 <= c < nc_:
                    eng.wait_ge(weighed, u0 + 8 * c + 8)
                    eng.activation(chunk(mix_hi, c), bank(5 + c % 2), ACT.Copy).then_inc(mix_hi_ready, 1)
                c, e = divmod(step - AHEAD[a], 8)
                if e == 0 and 0 <= c < nc_ - 1 and a == 2:
                    values(c + 1)
            if a == 0:
                for g in range(4):
                    eng.wait_ge(pool_ps, g + 1)
                    eng.activation(chunk(mix_hi, 4 + g), bank(4 + g), ACT.Copy, scale=column(vec, COL["pool_scale"] + g))\
                        .then_inc(mix_hi_ready, 1)

        def attention_dve(eng, a, link):
            at_, units = ATTENTIONS[a], ATTENTIONS[a]["units"]
            u0, nc_ = at_["u0"], at_["heads"] // 2
            eng.wait_ge(evacuated, projected(a))
            eng.wait_ge(const_landed, 16 * (a + 1))
            if a == 0:
                eng.wait_ge(sink_landed, 16)
                link(eng.tensor_scalar(neg_sink, sink_col, -1.0, None, ALU.mult))
                eng.memset(gate[:, :], 1.0)
                link(eng.memset(csum[:, 0:PAD + 1], 0.0))

            def rotated(out, plain, turned, done, count):
                link(eng.tensor_tensor(rot_a[:, :], plain, cos, ALU.mult))
                link(eng.tensor_tensor(rot_b[:, :], turned, sin, ALU.mult))
                eng.tensor_tensor(out, rot_a[:, :], rot_b[:, :], ALU.add).then_inc(done, 1)
                eng.wait_ge(done, count)

            def rotate(c):
                eng.wait_ge(rope_ps, 6 * a + 2 + c + 1)
                rotated(chunk(proj, at_["q"] + c), chunk(proj, at_["q"] + c), bank(7), rope_done, 4 * a + c + 1)

            def window_sums(g):
                if g:
                    eng.wait_ge(csum_used, g)
                u = chunk(proj, 6 + g)
                link(eng.tensor_tensor_scan(csum[:, PAD + 1:PAD + 1 + T], gate[:, :], u, 0.0, ALU.mult, ALU.add))
                eng.tensor_copy(csum[:, PAD + 1 + T:], csum[:, PAD + T:PAD + T + 1].to_broadcast([P, PAD])).then_inc(csum_done, 1)

            if a < 2:
                for g in range(2):
                    eng.wait_ge(rope_ps, 6 * a + g + 1)
                    rotated(chunk(kdup, g), bank(7 - 2 * g), bank(6 - 2 * g), kdup_done, 2 * a + g + 1)
                rotate(0)
            for step in range(len(units) + LAG_MIX + 1):
                u = step - LAG_N
                if 0 <= u < len(units):
                    c, hh, n, lo, nk = units[u]
                    k = stat_col(c, hh, n)
                    eng.wait_ge(probs, u0 + u + 1)
                    link(eng.reciprocal(INV[:, k], ROW[:, k]))
                    p = prob[a][u % 5][:, 0:nk * P]
                    eng.tensor_scalar(p, p, INV[:, k], None, ALU.mult).then_inc(probs_normed, 1)
                if step < len(units):
                    c, hh, n, lo, nk = units[step]
                    k = stat_col(c, hh, n)
                    eng.wait_ge(scores_ps, u0 + step + 1)
                    if step >= 3:
                        eng.wait_ge(probs, u0 + step - 2)
                    if a == 2 and n == 0:
                        eng.wait_ge(bias_ready, 2 * c + hh + 1)
                    s = 8 * a + 2 * c + hh
                    if a < 2:
                        eng.tensor_copy(score[a][step % 3][:, nk * P:nk * P + 1], neg_sink[:, s:s + 1])
                    eng.tensor_tensor_reduce(out=score[a][step % 3][:, 0:nk * P], in0=bank(step % 3)[:, 0:nk * P],
                                             in1=key_bias(a, c, hh, n, lo, nk), scale=-0.125,
                                             scalar=neg_sink[:, s:s + 1] if a < 2 else 3e38, op0=ALU.add, op1=ALU.min,
                                             accum_out=NEG[:, k]).then_inc(neg_max, 1)
                c, e = divmod(step - 7 - LAG_MIX, 8)
                if e == 0 and 0 <= c < nc_:
                    eng.wait_ge(mix_hi_ready, KD * a + c + 1)
                    eng.tensor_tensor(chunk(mix_lo, c), bank(5 + c % 2), chunk(mix_hi, c).bitcast(F32), ALU.subtract)\
                        .then_inc(mix_ready, 1)
                c, e = divmod(step - AHEAD[a], 8)
                if e == 0 and 0 <= c < nc_ - 1 and a < 2:
                    rotate(c + 1)
                if a == 0 and step % 8 == 2 and step // 8 < 4:
                    window_sums(step // 8)
            if a == 0:
                for g in range(4):
                    eng.wait_ge(mix_hi_ready, 4 + g + 1)
                    eng.scalar_tensor_tensor(chunk(mix_lo, 4 + g), bank(4 + g), column(vec, COL["pool_scale"] + g),
                                             chunk(mix_hi, 4 + g).bitcast(F32), ALU.mult, ALU.subtract).then_inc(mix_ready, 1)

        def pool_gpsimd(eng):
            for g, w in enumerate(POOL_WINDOWS):
                half = w // 2
                eng.wait_ge(csum_done, g + 1)
                eng.wait_ge(tab_landed, 32)
                eng.tensor_tensor(pool_e[:, :], csum[:, PAD + half:PAD + half + T + 1], csum[:, PAD - half:PAD - half + T + 1],
                                  ALU.subtract).then_inc(csum_used, 1)
                eng.wait_ge(csum_used, g + 1)
                eng.tensor_tensor(pool_e[:, :], pool_e[:, :], ptab[:, g * TAIL:g * TAIL + T + 1], ALU.mult).then_inc(pool_step, 1)
                eng.wait_ge(pool_step, 2 * g + 1)
                eng.tensor_tensor(pool_d[g][:, :], pool_e[:, 0:T], pool_e[:, 1:T + 1], ALU.add).then_inc(pool_step, 1)
                eng.wait_ge(pool_step, 2 * g + 2)
                eng.tensor_tensor(pool_d[g][:, :], pool_d[g][:, :], chunk(proj, 6 + g), ALU.subtract).then_inc(pool_diff, 1)

        def skewed(hd):
            return skew[hd, 0:5 * P * P].rearrange("(p w) -> p w", w=5 * P)[:, P - 1:P - 1 + T]

        def bias_gpsimd(eng):
            for hd in range(16):
                k = hd % 2
                if hd == 0:
                    eng.wait_ge(table_landed, 64)
                    eng.wait_ge(const_landed, 48)
                if hd >= 2:
                    eng.wait_ge(neg_max, ATTENTIONS[2]["u0"] + 4 * (hd - 1))
                eng.dma_start(biases[k][:, :], skewed(hd))\
                    .then_inc(bias_landed[k], 16)
                eng.wait_ge(bias_landed[k], 16 * (hd // 2 + 1))
                eng.tensor_scalar(biases[k][:, :], biases[k][:, :], 8.0, None, ALU.mult).then_inc(bias_scaled, 1)
                eng.wait_ge(bias_scaled, hd + 1)
                own = biases[k][:, 3 * P:T]
                eng.tensor_tensor(own, own, mask[:, 0:P], ALU.add).then_inc(bias_ready, 1)

        def state_col(b):
            return slice((b - 1) * P, b * P)

        def hgrn_transpose(pe, src):
            for hd in range(4):
                for n in range(NB):
                    ins = pe.transpose(bank(4 + hd)[:, n * P:(n + 1) * P], src[:, hd * T + n * P:hd * T + (n + 1) * P], ident)
                ins.then_inc(hg_tp, 1)

        def hgrn_pe(pe):
            pe.wait_ge(mix_ready, KD + 4)
            pe.wait_ge(hg_q, 3)

            def mean_square(hd):
                pe.wait_ge(hg_osq, hd + 1)
                for n in range(NB):
                    ins = pe.matmul(bank(7)[:, n:n + 1], osq[:, n * P:(n + 1) * P], mean_head[:, 0:1], start=True, stop=True)
                ins.then_inc(hg_ms, 1)

            def spread_root(hd):
                pe.wait_ge(hg_diag, hd + 1)
                pe.matmul(bank(7), mean_head, gated[:, :], start=True, stop=True).then_inc(hg_spread, 1)

            def products(hd):
                for n in range(NB):
                    w = slice(hd * T + n * P, hd * T + (n + 1) * P)
                    ins = pe.matmul(bank(0)[:, n * P:(n + 1) * P], hc[:, w], hq[:, w], start=True, stop=True)
                ins.then_inc(hg_s_ps, 1)

            def updates(hd):
                for b in range(NHB - 1):
                    grp, r = divmod(b, 4)
                    w = slice(hd * T + grp * P, hd * T + (grp + 1) * P)
                    rows = slice(32 * r, 32 * r + 32)
                    ins = pe.matmul(bank(1 + r)[:, grp * P:(grp + 1) * P], hf[rows, w], hv[rows, w], start=True, stop=True)
                ins.then_inc(hg_u_ps, 1)

            products(0)
            updates(0)
            for hd in range(4):
                o = bank(5 + hd % 2)
                if hd >= 2:
                    pe.wait_ge(hg_norm, hd - 1)
                if hd:
                    mean_square(hd - 1)
                pe.wait_ge(hg_s, hd + 1)
                for n in range(NB):
                    pe.matmul(o[:, n * P:(n + 1) * P], hv[:, hd * T + n * P:hd * T + (n + 1) * P],
                              s_t[:, (hd % 2) * T + n * P:(hd % 2) * T + (n + 1) * P], start=n == 0, stop=False,
                              skip_group_check=True)
                if hd < 3:
                    products(hd + 1)
                for b in range(1, NHB):
                    if hd and b == NHB // 2:
                        spread_root(hd - 1)
                    pe.wait_ge(hg_state, (NHB - 1) * hd + b)
                    w = slice(b * HGRN_BLOCK, (b + 1) * HGRN_BLOCK)
                    ins = pe.matmul(o[:, w], state[hd % 2][:, state_col(b)], chunk(hq, hd)[:, w], start=False,
                                    stop=b == NHB - 1, skip_group_check=True)
                ins.then_inc(hg_o, 1)
                if hd < 3:
                    updates(hd + 1)
            pe.wait_ge(hg_norm, 3)
            mean_square(3)
            spread_root(3)

        def hgrn_prepare_act(eng, p):
            made = BY["in2"].g0 + p + 1
            if p == 1:
                eng.wait_ge(lb_ready, 1)
                eng.activation(lb_e, lb_m, ACT.Exp).then_inc(hg_lb, 1)
                eng.wait_ge(evacuated, made)
                eng.activation(hk[:, :], hf, ACT.Sigmoid).then_inc(hg_sig, 1)
            if p == 2:
                eng.wait_ge(hg_f, 2)
                eng.activation(hf, hf, ACT.Ln).then_inc(hg_ln, 1)
            if p == 3:
                eng.wait_ge(hg_diff, 1)
                eng.activation(hf, hf, ACT.Exp).then_inc(hg_exp, 1)
                eng.activation(he[:, :], hc[:, :], ACT.Exp).then_inc(hg_exp, 1)
                eng.wait_ge(hg_exp, 2)
                eng.activation(hc[:, :], hc[:, :], ACT.Exp, scale=-1.0).then_inc(hg_exp, 1)
            if p == 6:
                eng.wait_ge(evacuated, made)
                eng.activation(hg, hg, ACT.Silu).then_inc(hg_sig, 1)
            if p == 9:
                for hd in range(4):
                    eng.wait_ge(hg_tp, 5 + hd)
                    eng.activation(chunk(hv, hd), bank(4 + hd), ACT.Copy).then_inc(hg_ta, 1)

        def hgrn_act(eng):
            def split(hd):
                eng.wait_ge(hg_norm, hd + 1)
                eng.activation(chunk(mix_hi, 4 + hd), up[:, :], ACT.Copy).then_inc(mix_hi_ready, 1)

            for hd in range(4):
                eng.wait_ge(hg_o, hd + 1)
                if hd:
                    eng.wait_ge(hg_ms, hd)
                eng.activation(osq[:, :], bank(5 + hd % 2), ACT.Square).then_inc(hg_osq, 1)
                if hd:
                    split(hd - 1)
                eng.wait_ge(hg_ms, hd + 1)
                eng.activation(std4, bank(7)[:, 0:NB], ACT.Sqrt, bias=lbs[:, 31:32]).then_inc(hg_std, 1)
            split(3)

        def hgrn_prepare_dve(eng, p, link):
            if p == 0:
                l0 = COL["hgrn_lb_logits_2"]
                lb0, lb1 = vec[:, l0:l0 + 4], vec[:, l0 + 4:l0 + 8]
                link(eng.tensor_tensor(lb_s[:, 0:4], lb0, lb1, ALU.max))
                eng.tensor_tensor(lb_m[:, 0:4], lb0, lb_s[:, 0:4], ALU.subtract)
                eng.tensor_tensor(lb_m[:, 4:8], lb1, lb_s[:, 0:4], ALU.subtract).then_inc(lb_ready, 1)
                link(eng.memset(reset[:, :], 1.0))
                link(eng.memset(reset[:, 0:T:HGRN_BLOCK], 0.0))
            if p == 1:
                eng.wait_ge(hg_lb, 1)
                link(eng.tensor_tensor(lb_s[:, 0:4], lb_e[:, 0:4], lb_e[:, 4:8], ALU.add))
                link(eng.reciprocal(lb_s[:, 4:8], lb_s[:, 0:4]))
                link(eng.tensor_tensor(lb[:, 0:4], lb_e[:, 0:4], lb_s[:, 4:8], ALU.mult))
                link(eng.tensor_scalar(lb_rest[:, 0:4], lb[:, 0:4], -1.0, 1.0, ALU.mult, ALU.add))
                eng.wait_ge(hg_sig, 1)
                for hd in range(4):
                    ins = eng.tensor_scalar(chunk(hf, hd), chunk(hk, hd), lb_rest[:, hd:hd + 1], lb[:, hd:hd + 1], ALU.mult, ALU.add)
                ins.then_inc(hg_f, 1)
                eng.wait_ge(hg_f, 1)
                eng.tensor_scalar(hk[:, :], hf, -1.0, 1.0, ALU.mult, ALU.add).then_inc(hg_f, 1)
            if p == 2:
                eng.wait_ge(hg_ln, 1)
                for hd in range(4):
                    ins = eng.tensor_tensor_scan(chunk(hc, hd), reset[:, :], chunk(hf, hd), 0.0, ALU.mult, ALU.add)
                ins.then_inc(hg_cum, 1)
                eng.wait_ge(hg_cum, 1)
                cum = hc[:, :].rearrange("p (b l) -> p b l", l=HGRN_BLOCK)
                eng.tensor_tensor(hf.rearrange("p (b l) -> p b l", l=HGRN_BLOCK),
                                  cum[:, :, HGRN_BLOCK - 1:HGRN_BLOCK].to_broadcast([P, 4 * NHB, HGRN_BLOCK]), cum,
                                  ALU.subtract).then_inc(hg_diff, 1)
            if p == 3:
                eng.wait_ge(hg_exp, 1)
                eng.tensor_tensor(hf, hk[:, :], hf, ALU.mult).then_inc(hg_kend, 1)
                eng.wait_ge(hg_exp, 2)
                eng.wait_ge(evacuated, BY["in2"].g0 + p + 1)
                eng.tensor_tensor(hq, hq, he[:, :], ALU.mult).then_inc(hg_q, 1)
                eng.tensor_copy(decay, he[:, HGRN_BLOCK - 1::HGRN_BLOCK]).then_inc(hg_q, 1)
            if p == 4:
                eng.wait_ge(hg_exp, 3)
                eng.tensor_tensor(hc[:, :], hk[:, :], hc[:, :], ALU.mult).then_inc(hg_q, 1)
            if p == 5:
                for hd in range(4):
                    eng.wait_ge(hg_tp, 1 + hd)
                    eng.tensor_copy(chunk(hf, hd), bank(4 + hd)).then_inc(hg_tb, 1)

        def hgrn_dve(eng, link):
            causal = mask[:, 2 * P:3 * P].bitcast(U32)
            link(eng.memset(s_t[:, :], 0.0))

            def within(hd):
                eng.wait_ge(hg_s_ps, hd + 1)
                st4 = chunk(s_t, hd % 2).rearrange("p (n l) -> p n l", l=P)
                eng.copy_predicated(st4, causal[:, None, :].to_broadcast([P, NB, P]), bank(0).rearrange("p (n l) -> p n l", l=P))\
                    .then_inc(hg_s, 1)

            def root_diagonal(hd):
                eng.wait_ge(hg_std, hd + 1)
                link(eng.reciprocal(inv4, std4))
                eng.scalar_tensor_tensor(gated[:, :].rearrange("p (n t) -> p n t", t=P), ident[:, None, :].to_broadcast([P, NB, P]),
                                         float(P), inv4[:, :, None].to_broadcast([P, NB, P]), ALU.mult, ALU.mult)\
                    .then_inc(hg_diag, 1)

            def normed(hd):
                eng.wait_ge(hg_spread, hd + 1)
                link(eng.tensor_copy(gate[:, :], bank(7)))
                link(eng.scalar_tensor_tensor(prod[:, :], bank(5 + hd % 2), column(vec, COL["hgrn_norm_w_2"] + hd), gate[:, :],
                                              ALU.mult, ALU.mult))
                eng.wait_ge(hg_sig, 2)
                eng.wait_ge(mix_ready, KD + 4 + hd)
                eng.tensor_tensor(up[:, :], prod[:, :], chunk(hg, hd), ALU.mult).then_inc(hg_norm, 1)
                eng.wait_ge(mix_hi_ready, KD + 4 + hd + 1)
                eng.tensor_tensor(chunk(mix_lo, 4 + hd), up[:, :], chunk(mix_hi, 4 + hd).bitcast(F32), ALU.subtract)\
                    .then_inc(mix_ready, 1)

            within(0)
            for hd in range(4):
                eng.wait_ge(hg_u_ps, hd + 1)
                if hd >= 2:
                    eng.wait_ge(hg_o, hd - 1)
                for b in range(NHB - 1):
                    grp, r = divmod(b, 4)
                    add = bank(1 + r)[:, grp * P:(grp + 1) * P]
                    to = state[hd % 2][:, state_col(b + 1)]
                    if hd and b == 3:
                        root_diagonal(hd - 1)
                    if b == 0:
                        eng.tensor_copy(to, add).then_inc(hg_state, 1)
                    else:
                        eng.wait_ge(hg_state, (NHB - 1) * hd + b)
                        eng.scalar_tensor_tensor(to, state[hd % 2][:, state_col(b)], decay[:, NHB * hd + b:NHB * hd + b + 1], add,
                                                 ALU.mult, ALU.add).then_inc(hg_state, 1)
                if hd < 3:
                    within(hd + 1)
                if hd:
                    normed(hd - 1)
            root_diagonal(3)
            normed(3)

        block = ctx.enter_context(nc.Block())

        def wait_act(eng, sem, count):
            if not isinstance(count, int):
                count = eng.to_reg(count)
                eng.wait_ge(vec_landed, 32)
            wait(eng, sem, count)

        @block.sync
        def _(sp):
            sp.dma_start(vec[:, :], vecs).then_inc(vec_landed, 16)
            sp.dma_start(small[:, :], small_consts).then_inc(vec_landed, 16)
            for st in stages:
                src = weights[st.name]

                def load(i, s, st=st, src=src):
                    per = 2 if st.kind == "in" else 4
                    slot = (st.q0 + s) % 2
                    wait(sp, lo_rounded, st.q0 + s - 1 + per * i)
                    if st.kind == "in":
                        n = PAIR
                        a = src[i * 2 + s] if isinstance(i, int) else src[bass.ds(i * 2 + s, 1)].rearrange("a p w -> (a p) w")
                    else:
                        m = i * 2 + s // 2
                        c0, n = ((0, 12 * P), (12 * P, 10 * P))[s % 2]
                        a = src[m] if isinstance(i, int) else src[bass.ds(m, 1)].rearrange("a p w -> (a p) w")
                        a = a[:, c0:c0 + n]
                    sp.dma_start(raw[:, slot * PAIR:slot * PAIR + n], a).then_inc(raw_landed[slot], 16)
                    if st.q0 == 0 and s == 0 and isinstance(i, int) and i == 0:
                        w = KD * T // X_LOADS
                        for j in range(X_LOADS):
                            sp.dma_start(h[:, j * w:(j + 1) * w], x_t[:, j * w:(j + 1) * w]).then_inc(x_landed[j], 16)

                if st.kind == "in":
                    def body(i, load=load, u=2):
                        for s in range(u):
                            load(i, s)
                    repeat(sp, st.pairs // 2, body, first=1 if st.q0 == 0 else 0)
                    if st.pairs % 2:
                        body(st.pairs // 2, u=1)
                else:
                    def body(i, load=load):
                        for s in range(4):
                            load(i, s)
                    repeat(sp, KD // 2, body)

        @block.tensor
        def _(pe):
            def keep_warm(n):
                for _ in range(n):
                    pe.matmul(bank(WARM_BANK)[:, 0:2 * P], mean_d, small[:, 0:2 * P], start=True, stop=True)

            pe.wait_ge(vec_landed, 32)
            keep_warm(10)

            def mean_squares(r):
                pe.wait_ge(vec_landed, 32)
                pe.wait_ge(ssum_ready, KD * (r + 1))
                for n in range(NB):
                    ins = pe.matmul(bank(STATS_BANK)[:, n:n + 1], ssum[:, n * P:(n + 1) * P], mean_d[:, 0:1], start=True, stop=True)
                ins.then_inc(ms_ready, 1)

            def spread_roots(r):
                pe.wait_ge(diag_ready, r + 1)
                pe.matmul(bank(STATS_BANK), mean_d, rstd[:, :], start=True, stop=True).then_inc(spread, 1)

            def product(b, hi, lo, rhs_hi, rhs_lo, start, stop):
                pe.matmul(bank(b), hi, rhs_hi, start=start, stop=False)
                pe.matmul(bank(b), hi, rhs_lo, start=False, stop=False)
                return pe.matmul(bank(b), lo, rhs_hi, start=False, stop=stop)

            def tile_of(w, slot, t):
                return w[:, slot * PAIR + t * P:slot * PAIR + (t + 1) * P]

            for st in stages:
                if st.name == "out1":
                    attention_pe(pe, 0)
                if st.name == "out2":
                    attention_pe(pe, 1)
                    hgrn_pe(pe)
                if st.name == "out3":
                    attention_pe(pe, 2)
                if st.kind == "in":
                    mixed = st.evac in ("add", "hold")
                    r_hi, r_lo = (mix_hi, mix_lo) if mixed else (x_split[:, 0:KD * T], x_split[:, KD * T:])
                    ready = (mix_ready, KD * ("out1", "out2", "out3").index(st.name)) if mixed else (x_ready, KD * st.x_index)

                    stats_at = 2 if st.name in ("up1", "in1", "up2") else 4

                    def body(i, u=2, st=st, r_hi=r_hi, r_lo=r_lo, ready=ready, mixed=mixed, stats_at=stats_at):
                        for s in range(u):
                            slot, pair_bank = (st.q0 + s) % 2, (st.g0 + s) % 2
                            wait(pe, lo_rounded, st.q0 + s + 1 + 2 * i)
                            wait(pe, evacuated, st.g0 + s - 1 + 2 * i)
                            for k in range(KD):
                                if s == 0:
                                    wait(pe, ready[0], ready[1] + k + 1)
                                for t in range(2):
                                    last = product(2 * pair_bank + t, tile_of(w_hi, slot, t * KD + k),
                                                   tile_of(w_lo, slot, t * KD + k), chunk(r_hi, k), chunk(r_lo, k),
                                                   k == 0, k == KD - 1)
                                if s == 1 and isinstance(i, int) and i == 0 and not mixed:
                                    if k == stats_at:
                                        mean_squares(st.stat)
                                    if k == stats_at + 2:
                                        spread_roots(st.stat)
                            last.then_inc(pair_done, 1)
                    if st.name == "in2":
                        repeat(pe, 3, body, first=1)
                        pe.wait_ge(hg_kend, 1)
                        hgrn_transpose(pe, hf)
                        for i in (3, 4):
                            body(i)
                        pe.wait_ge(hg_tb, 4)
                        hgrn_transpose(pe, hv)
                        body(5, u=1)
                        pe.wait_ge(hg_ta, 4)
                        continue
                    repeat(pe, st.pairs // 2, body, first=1)
                    if st.pairs % 2:
                        body(st.pairs // 2, u=1)
                else:
                    a0 = KF * ("down1", "down2", "down3", "down4").index(st.name)

                    def body(i, st=st, a0=a0):
                        for mm in range(2):
                            b = 2 * ((st.g0 + mm) % 2)
                            wait(pe, evacuated, st.g0 + mm - 1 + 2 * i)
                            f = 0
                            for half in range(2):
                                s = 2 * mm + half
                                slot = (st.q0 + s) % 2
                                wait(pe, lo_rounded, st.q0 + s + 1 + 4 * i)
                                if mm == 0:
                                    wait(pe, act_ready, a0 + sum(HALF_TILES[:half + 1]))
                                for t in range(HALF_TILES[half]):
                                    last = product(b, tile_of(w_hi, slot, t), tile_of(w_lo, slot, t),
                                                   chunk(act, f), chunk(act, KF + f), f == 0, f == KF - 1)
                                    f += 1
                                last.then_inc(pair_done, 1)
                    repeat(pe, KD // 2, body)
                if st.name in BARRIERS:
                    keep_warm(5 if st.kind == "down" else 8)
                    mean_squares(st.stat)
                    keep_warm(3)
                    spread_roots(st.stat)
                    if st is not stages[-1]:
                        keep_warm(8)

        def round_weights(eng, q, i, per):
            slot = q % 2
            wait(eng, raw_landed[slot], 16 * (q // 2 + 1) + 8 * per * i)
            wait(eng, pair_done, q - 1 + per * i)
            n = PAIR_TILES[q] * P
            w = slice(slot * PAIR, slot * PAIR + n)
            eng.activation(w_hi[:, w], raw[:, w], ACT.Copy).then_inc(hi_rounded, 1)

        def rest_weights(eng, q, i, per):
            slot = q % 2
            wait(eng, hi_rounded, q + 1 + per * i)
            n = PAIR_TILES[q] * P
            w = slice(slot * PAIR, slot * PAIR + n)
            eng.tensor_tensor(w_lo[:, w], raw[:, w], w_hi[:, w].bitcast(F32), ALU.subtract).then_inc(lo_rounded, 1)

        def square(eng, r, m, src, parity):
            wait_act(eng, ssum_ready, KD * r + m - 1)
            eng.activation(chunk(sq, parity), src, ACT.Square).then_inc(sq_ready, 1)

        def add_square(eng, r, m, parity):
            wait(eng, sq_ready, KD * r + m + 1)
            wait(eng, ssum_ready, KD * r + m)
            eng.tensor_tensor(ssum[:, :], ssum[:, :], chunk(sq, parity), ALU.add).then_inc(ssum_ready, 1)

        def square_apart(eng, r, m):
            eng.activation(chunk(squares, m), chunk(h, m), ACT.Square).then_inc(sq_ready, 1)

        def sum_squares(eng, r, link):
            eng.wait_ge(sq_ready, KD * (r + 1))
            half = KD * T // 2
            while half > T:
                link(eng.tensor_tensor(squares[:, 0:half], squares[:, 0:half], squares[:, half:2 * half], ALU.add))
                half //= 2
            eng.tensor_tensor(ssum[:, :], squares[:, 0:T], squares[:, T:2 * T], ALU.add).then_inc(ssum_ready, KD)

        def round_x(eng, n, m, col):
            eng.activation(chunk(x_split, m), chunk(h, m), ACT.Copy, scale=column(vec, col + m)).then_inc(x_hi_ready, 1)

        def rest_x(eng, n, m, col):
            wait(eng, x_hi_ready, KD * n + m + 1)
            eng.scalar_tensor_tensor(chunk(x_split, KD + m), chunk(h, m), column(vec, col + m),
                                     chunk(x_split, m).bitcast(F32), ALU.mult, ALU.subtract).then_inc(x_ready, 1)

        @block.scalar
        def _(eng):
            def root(r):
                wait(eng, ms_ready, r + 1)
                eng.activation(std4, bank(STATS_BANK)[:, 0:NB], ACT.Sqrt, bias=lbs[:, 31:32]).then_inc(std_ready, 1)

            eng.wait_ge(vec_landed, 32)
            eng.activation(tiny[:, 250:251], vec[:, 0:1], ACT.Copy)
            round_weights(eng, 0, 0, 0)
            for m in range(KD):
                if m % (KD // X_LOADS) == 0:
                    eng.wait_ge(x_landed[m // (KD // X_LOADS)], 16)
                round_x(eng, 0, m, COL["ffn1_norm"])
            for m in range(KD):
                square_apart(eng, 0, m)
            round_weights(eng, 1, 0, 0)

            for st in stages:
                if st.name == "out1":
                    attention_act(eng, 0)
                if st.name == "out2":
                    attention_act(eng, 1)
                    hgrn_act(eng)
                if st.name == "out3":
                    attention_act(eng, 2)
                if st.kind == "in" and st.evac in ("silu", "conv", "project"):
                    round_weights(eng, st.q0 + 2, 0, 0)
                    root(st.stat)
                f0 = KF * ("up1", "up2", "up3", "up4").index(st.name) if st.name.startswith("up") else 0

                def next_weights(i, s, per, st=st):
                    if isinstance(i, int) and st.q0 + s + per * i + 2 >= last_pair:
                        pass
                    elif isinstance(i, int) and st.name in BARRIERS and s + per * i == st.pairs - 1:
                        pass
                    elif isinstance(i, int) and i == 0 and s == 0 and st.evac in ("silu", "conv", "project"):
                        pass
                    elif isinstance(i, int):
                        round_weights(eng, st.q0 + s + per * i + 2, 0, 0)
                    else:
                        round_weights(eng, st.q0 + s + 2, i, per)

                def pair_step(i, s, per, st=st, f0=f0):
                    f = s + 2 * i
                    if st.evac in ("silu", "conv"):
                        next_weights(i, s, per)
                        wait(eng, gate_ready, f0 + 1 + f)
                        eng.activation(gated[:, :], gate[:, :], ACT.Silu if st.evac == "silu" else ACT.Gelu)\
                            .then_inc(gated_ready, 1)
                    if st.evac in ("add", "hold"):
                        if st.kind == "in":
                            ms, g = [2 * s + 4 * i, 2 * s + 1 + 4 * i], st.g0 + s + 2 * i
                        else:
                            ms, g = ([s // 2 + 2 * i], st.g0 + s // 2 + 2 * i) if s % 2 else ([], 0)
                        for k, m in enumerate(ms):
                            if k == 0:
                                wait_act(eng, evacuated, g + 1)
                            parity = k if st.kind == "in" else s // 2
                            if st.x_index is not None:
                                round_x(eng, st.x_index, m, st.next_norm)
                            square(eng, st.stat, m, chunk(h if st.evac == "add" else y, m), parity)
                    if st.evac not in ("silu", "conv"):
                        next_weights(i, s, per)
                    if st.evac in ("silu", "conv"):
                        wait_act(eng, prod_ready, f0 + 1 + f)
                        eng.activation(chunk(act, f), prod[:, :], ACT.Copy).then_inc(prod_hi, 1)

                if st.kind == "in":
                    def body(i, u=2, st=st):
                        for s in range(u):
                            pair_step(i, s, 2)
                            if st.name == "in2":
                                hgrn_prepare_act(eng, 2 * i + s)
                    repeat(eng, st.pairs // 2, body, first=5 if st.name == "in2" else int(st.evac != "hold"), last=1)
                    if st.pairs % 2:
                        body(st.pairs // 2, u=1)
                else:
                    def body(i):
                        for s in range(4):
                            pair_step(i, s, 4)
                    repeat(eng, KD // 2, body, last=1)

                if st.name in BARRIERS:
                    bar = BARRIERS[st.name]
                    root(st.stat)
                    if bar["x_index"] is not None:
                        for m in range(KD):
                            wait(eng, h_ready, bar["h0"] + m + 1)
                            round_x(eng, bar["x_index"], m, bar["next_col"])
                            square_apart(eng, bar["stat"], m)
                            if m == KD // 2 and st is not stages[-1]:
                                round_weights(eng, st.q0 + st.pairs + 1, 0, 0)

        @block.vector
        def _(eng):
            steps = [0]

            def link(ins):
                steps[0] += 1
                ins.then_inc(dve_step, 1)
                eng.wait_ge(dve_step, steps[0])

            def inverse(r):
                wait(eng, std_ready, r + 1)
                link(eng.reciprocal(inv4, std4))
                eng.scalar_tensor_tensor(rstd[:, :].rearrange("p (n t) -> p n t", t=P), ident[:, None, :].to_broadcast([P, NB, P]),
                                         float(D), inv4[:, :, None].to_broadcast([P, NB, P]), ALU.mult, ALU.mult)\
                    .then_inc(diag_ready, 1)
                wait(eng, spread, r + 1)

            eng.memset(lbs[:, :], EPS)
            link(eng.memset(shifted[:, 0:2], 0.0))
            rest_weights(eng, 0, 0, 0)
            for m in range(KD):
                rest_x(eng, 0, m, COL["ffn1_norm"])
            sum_squares(eng, 0, link)
            rest_weights(eng, 1, 0, 0)

            for st in stages:
                if st.name == "out1":
                    attention_dve(eng, 0, link)
                if st.name == "out2":
                    attention_dve(eng, 1, link)
                    hgrn_dve(eng, link)
                if st.name == "out3":
                    attention_dve(eng, 2, link)
                if st.kind == "in" and st.evac in ("silu", "conv", "project"):
                    rest_weights(eng, st.q0 + 2, 0, 0)
                    inverse(st.stat)
                    eng.tensor_copy(rstd[:, :], bank(STATS_BANK)).then_inc(rstd_ready, 1)
                    eng.wait_ge(rstd_ready, ("up1", "in1", "up2", "in2", "up3", "in3", "up4").index(st.name) + 1)
                if st.evac in ("add", "hold"):
                    link(eng.memset(ssum[:, :], 0.0))
                f0 = KF * ("up1", "up2", "up3", "up4").index(st.name) if st.name.startswith("up") else 0
                conv0 = KF * (st.name == "up4")
                layer = int(st.name == "up4")

                def next_weights(i, s, per, st=st):
                    if isinstance(i, int) and st.q0 + s + per * i + 2 >= last_pair:
                        pass
                    elif isinstance(i, int) and st.name in BARRIERS and s + per * i == st.pairs - 1:
                        pass
                    elif isinstance(i, int) and i == 0 and s == 0 and st.evac in ("silu", "conv", "project"):
                        pass
                    elif isinstance(i, int):
                        rest_weights(eng, st.q0 + s + per * i + 2, 0, 0)
                    else:
                        rest_weights(eng, st.q0 + s + 2, i, per)

                def pair_step(i, s, per, st=st, f0=f0, conv0=conv0, layer=layer):
                    f = s + 2 * i
                    b = 2 * ((st.g0 + s) % 2) if st.kind == "in" else 2 * ((st.g0 + s // 2) % 2)
                    done = st.q0 + s + 1 + per * i
                    if st.evac in ("silu", "conv"):
                        wait(eng, pair_done, done)
                        if st.evac == "silu":
                            eng.tensor_tensor(gate[:, :], bank(b), rstd[:, :], ALU.mult).then_inc(gate_ready, 1)
                            eng.tensor_tensor(up[:, :], bank(b + 1), rstd[:, :], ALU.mult).then_inc(evacuated, 1)
                        else:
                            eng.tensor_tensor(shifted[:, 2:], bank(b), rstd[:, :], ALU.mult).then_inc(u_ready, 1)
                            eng.tensor_tensor(up[:, :], bank(b + 1), rstd[:, :], ALU.mult).then_inc(evacuated, 1)
                            cw = COL["ffn_conv_w_2"] + layer * 3 * KF
                            tap = [column(vec, cw + j * KF + f) for j in range(3)]
                            cb = column(vec, COL["ffn_conv_b_2"] + layer * KF + f)
                            wait(eng, u_ready, conv0 + 1 + f)
                            eng.tensor_scalar(prod[:, :], shifted[:, 2:], tap[2], cb, ALU.mult, ALU.add)\
                                .then_inc(conv_a, 1)
                            wait(eng, conv_a, conv0 + 1 + f)
                            eng.scalar_tensor_tensor(gate[:, :], shifted[:, 1:T + 1], tap[1], prod[:, :], ALU.mult, ALU.add)\
                                .then_inc(conv_b, 1)
                            wait(eng, conv_b, conv0 + 1 + f)
                            eng.scalar_tensor_tensor(gate[:, :], shifted[:, 0:T], tap[0], gate[:, :], ALU.mult, ALU.add)\
                                .then_inc(gate_ready, 1)
                        next_weights(i, s, per)
                        wait(eng, gated_ready, f0 + 1 + f)
                        wait(eng, evacuated, st.g0 + s + 1 + 2 * i)
                        eng.tensor_tensor(prod[:, :], gated[:, :], up[:, :], ALU.mult).then_inc(prod_ready, 1)
                    elif st.evac == "project":
                        wait(eng, pair_done, done)
                        out = chunk(proj, f, 2 * T).rearrange("p (a t) -> p a t", a=2)
                        both = bank(b, 2).rearrange("p (a t) -> p a t", a=2)
                        eng.tensor_tensor(out, both, rstd[:, None, :].to_broadcast([P, 2, T]), ALU.mult)\
                            .then_inc(evacuated, 1)
                    elif st.kind == "in" or s % 2:
                        wait_act(eng, pair_done, done)
                        ms = [2 * s + 4 * i, 2 * s + 1 + 4 * i] if st.kind == "in" else [s // 2 + 2 * i]
                        for k, m in enumerate(ms):
                            if st.evac == "add":
                                ins = eng.scalar_tensor_tensor(chunk(h, m), bank(b + k), st.factor, chunk(h, m), ALU.mult, ALU.add)
                            else:
                                ins = eng.tensor_copy(chunk(y, m), bank(b + k))
                        ins.then_inc(evacuated, 1)
                        for k, m in enumerate(ms):
                            if st.x_index is not None:
                                rest_x(eng, st.x_index, m, st.next_norm)
                            add_square(eng, st.stat, m, k if st.kind == "in" else s // 2)
                    if st.evac not in ("silu", "conv"):
                        next_weights(i, s, per)
                    if st.evac in ("silu", "conv"):
                        wait(eng, prod_hi, f0 + 1 + f)
                        eng.tensor_tensor(chunk(act, KF + f), prod[:, :], chunk(act, f).bitcast(F32), ALU.subtract)\
                            .then_inc(act_ready, 1)

                if st.kind == "in":
                    def body(i, u=2, st=st):
                        for s in range(u):
                            pair_step(i, s, 2)
                            if st.name == "in2":
                                hgrn_prepare_dve(eng, 2 * i + s, link)
                    repeat(eng, st.pairs // 2, body, first=5 if st.name == "in2" else int(st.evac != "hold"), last=1)
                    if st.pairs % 2:
                        body(st.pairs // 2, u=1)
                else:
                    def body(i):
                        for s in range(4):
                            pair_step(i, s, 4)
                    repeat(eng, KD // 2, body, last=1)

                if st.name in BARRIERS:
                    bar = BARRIERS[st.name]
                    inverse(st.stat)
                    inv_root = bank(STATS_BANK)
                    scaled = [gate, gated]
                    for m in range(KD + 2):
                        if m < KD:
                            if bar["kind"] == "final":
                                eng.scalar_tensor_tensor(chunk(h, m), chunk(h, m), column(vec, bar["col"] + m), inv_root,
                                                         ALU.mult, ALU.mult).then_inc(h_ready, 1)
                            else:
                                wait(eng, h_ready, bar["h0"] + m - 1)
                                eng.scalar_tensor_tensor(scaled[m % 2][:, :], chunk(y, m), column(vec, bar["col"] + m),
                                                         inv_root, ALU.mult, ALU.mult).then_inc(scaled_ready, 1)
                        if m >= 2 and bar["x_index"] is not None:
                            rest_x(eng, bar["x_index"], m - 2, bar["next_col"])
                    if bar["x_index"] is not None:
                        if st is not stages[-1]:
                            rest_weights(eng, st.q0 + st.pairs + 1, 0, 0)
                        sum_squares(eng, bar["stat"], link)

        @block.gpsimd
        def _(eng):
            eng.dma_start(sink_col, sinks.to_broadcast([P, 16])).then_inc(sink_landed, 16)
            eng.dma_start(scratch[:, 3 * P:5 * P], rel_bias[:, 1:257]).then_inc(table_landed, 16)
            eng.dma_start(tiny[0:16, 240:242], rel_bias[:, 0:2]).then_inc(table_landed, 16)
            eng.wait_ge(table_landed, 32)
            eng.tensor_copy(shifted[0:16, 2:2 + 3 * P], tiny[0:16, 240:241].to_broadcast([16, 3 * P])).then_inc(far_ready, 1)
            eng.wait_ge(far_ready, 1)
            eng.dma_start(scratch[:, 0:3 * P], shifted[0:16, 2:2 + 3 * P]).then_inc(table_landed, 16)
            eng.wait_ge(table_landed, 48)
            eng.dma_start(skew.rearrange("h (p w) -> h p w", w=5 * P + 1)[:, :, 0:5 * P],
                          scratch[:, None, :].to_broadcast([16, P, 5 * P])).then_inc(table_landed, 16)

            for st in stages:
                if st.evac == "project":
                    eng.wait_ge(pair_done, st.q0)
                    a = ("in1", "in2", "in3").index(st.name)
                    eng.dma_start(mconst[:, :], mixer_consts[a]).then_inc(const_landed, 16)
                    if a == 0:
                        eng.dma_start(ptab[:, :], pool_tab).then_inc(tab_landed, 16)
                        eng.dma_start(pw[:, :], pool_w).then_inc(tab_landed, 16)
                if st.name == "out1":
                    pool_gpsimd(eng)
                if st.name == "out3":
                    bias_gpsimd(eng)
                if st.name in BARRIERS and BARRIERS[st.name]["kind"] == "post":
                    bar = BARRIERS[st.name]
                    for m in range(KD):
                        wait(eng, scaled_ready, bar["h0"] - 8 + m + 1)
                        eng.tensor_tensor(chunk(h, m), chunk(h, m), (gate, gated)[m % 2][:, :], ALU.add).then_inc(h_ready, 1)
            if stop is not None:
                eng.wait_ge(evacuated, stages[-1].g0 + stages[-1].groups)
                if stages[-1].name in BARRIERS:
                    eng.wait_ge(h_ready, BARRIERS[stages[-1].name]["h0"] + KD)
                eng.dma_start(out_t, h[:, :]).then_inc(out_landed, 16)
                eng.wait_ge(out_landed, 16)
            else:
                for m in range(KD):
                    eng.wait_ge(h_ready, BARRIERS["down4"]["h0"] + m + 1)
                    eng.dma_start(out_t[:, m * T:(m + 1) * T], chunk(h, m)).then_inc(out_landed, 16)
                eng.wait_ge(out_landed, 16 * KD)


def lay_out(inputs):
    a = {k: np.asarray(v) for k, v in inputs.items()}
    feat = lambda v: v.reshape(-1, P).T
    x_t = a["x"][0].T.reshape(KD, P, T).transpose(1, 0, 2).reshape(P, KD * T)
    vecs = np.concatenate([feat(a[n].reshape(-1)) for n, _ in _VECS], axis=1)

    def tiles(w):
        k, m = w.shape
        return w.reshape(k // P, P, m // P, P).transpose(2, 1, 0, 3).reshape(m // P, P, k)

    def pairs(t):
        return t.reshape(-1, 2, P, t.shape[-1]).transpose(0, 2, 1, 3).reshape(-1, P, 2 * t.shape[-1])

    def twin(g, u):
        return pairs(np.stack([tiles(g), tiles(u)], axis=1).reshape(2 * KF, P, D))

    w = {}
    w["up1"] = twin(a["ffn1_w_gate"][0], a["ffn1_w_up"][0])
    w["down1"] = tiles(a["ffn1_w_down"][0])
    w["in1"] = pairs(tiles(a["w_in"][0]))
    w["out1"] = pairs(tiles(a["w_out"][0]))
    w["up2"] = twin(a["ffn2_w_gate"][0], a["ffn2_w_up"][0])
    w["down2"] = tiles(a["ffn2_w_down"][0])
    w["in2"] = pairs(tiles(a["even_w_in_2"][0])[IN2_ORDER])
    w["out2"] = pairs(tiles(a["even_w_out_2"][0]))
    w["up3"] = twin(a["ffn_w_up_2"][0][:, :F], a["ffn_w_up_2"][0][:, F:])
    w["down3"] = tiles(a["ffn_w_down_2"][0])
    w["in3"] = pairs(tiles(a["odd_w_in_2"][0]))
    w["out3"] = pairs(tiles(a["odd_w_out_2"][0]))
    w["up4"] = twin(a["ffn_w_up_2"][1][:, :F], a["ffn_w_up_2"][1][:, F:])
    w["down4"] = tiles(a["ffn_w_down_2"][1])
    arrays = {"x_t": x_t, "vecs": vecs, **{f"w_{n}": v for n, v in w.items()}}
    arrays["pool_w"] = a["pool_w"][0].transpose(1, 0, 2).reshape(P, 4 * P)
    arrays["sinks"] = np.concatenate([a["sink_logits"][0], a["even_sinks_2"][0]]).reshape(1, 16)
    arrays["rel_bias"] = a["odd_rel_bias_2"][0][:, ::-1]
    return arrays


def shape_constants():
    t = np.arange(T, dtype=np.float32)
    p = np.arange(P)
    eye = np.eye(P, dtype=np.float32)

    def rotary(theta, dim, head=64):
        half = dim // 2
        inv = (np.float32(theta) ** (-np.arange(0, dim, 2, dtype=np.float32) / np.float32(dim))).astype(np.float32)
        c, s, pm = np.ones((P, T), np.float32), np.zeros((P, T), np.float32), np.zeros((P, P), np.float32)
        for m in range(P):
            d = m % head
            if d < dim:
                ang = t * inv[d % half]
                c[m], s[m] = np.cos(ang), np.sin(ang)
                if d < half:
                    pm[m + half, m] = -1.0
                else:
                    pm[m - half, m] = 1.0
        return c, s, pm

    def picks(pm):
        sel = [np.zeros((P, P), np.float32) for _ in range(2)]
        for g in range(2):
            for m in range(P):
                sel[g][64 * g + m % 64, m] = 1.0
        return sel, [(s @ pm).astype(np.float32) for s in sel]

    q, k = p[:, None], np.arange(384)[None, :]
    neg = np.float32(-8 * BIG)
    m0 = np.where(np.abs(q + P - k) <= P, 0, neg)
    chunk_q, chunk_k = 2 + q // 64, np.arange(384)[None, :] // 64
    m1 = np.where((chunk_k <= chunk_q) & (chunk_k >= chunk_q - 2), 0, neg)
    m1[:, 256:384] = 0
    same = (p[:, None] // HGRN_BLOCK == p[None, :] // HGRN_BLOCK) & (p[:, None] <= p[None, :])
    m1[:, 256:384] = same
    m2 = np.zeros((P, 384))
    m2[:, 0:P] = np.where(p[None, :] // 64 <= p[:, None] // 64, 0, neg)
    mixers = []
    for (theta, dim), mk in (((500000.0, 16), m0), ((10000.0, 64), m1), ((10000.0, 64), m2)):
        c, s, pm = rotary(theta, dim)
        sel, selp = picks(pm)
        mixers.append(np.concatenate([c, s, mk.astype(np.float32), pm, *sel, *selp], axis=1))
    tab = np.zeros((4, TAIL), np.float32)
    for g, w in enumerate(POOL_WINDOWS):
        tt = np.arange(T + 1)
        n = np.minimum(tt + w // 2, T) - np.maximum(tt - w // 2, 0)
        tab[g, :T + 1] = 0.5 / n
    tab = np.broadcast_to(tab.reshape(1, -1), (P, 4 * TAIL))
    small = np.concatenate([eye, np.full((P, P), 1.0 / D, np.float32), np.full((P, P), 1.0 / P, np.float32)], axis=1)
    return {"mixer_consts": np.stack(mixers), "pool_tab": tab, "small_consts": small}


def kernel(**inputs):
    import concourse.bacc as bacc
    from concourse.bass_utils import run_bass_kernel_spmd as run

    nc = bacc.Bacc("TRN2", target_bir_lowering=False, num_devices=1)
    arrays = {**lay_out(inputs), **shape_constants()}
    arrays = {n: np.ascontiguousarray(v, dtype=None) for n, v in arrays.items()}
    ap = {n: nc.dram_tensor(f"in_{n}", v.shape, F32, kind="ExternalInput").ap() for n, v in arrays.items()}
    out_t = nc.dram_tensor("out_t", (P, KD * T), F32, kind="ExternalOutput").ap()
    scratch = nc.dram_tensor("scratch", (16, 5 * P), F32).ap()
    skew = nc.dram_tensor("skew", (16, P * (5 * P + 1)), F32).ap()
    build(nc, ap["x_t"], ap["vecs"], {s.name: ap[f"w_{s.name}"] for s in STAGES}, ap["mixer_consts"], ap["pool_tab"],
          ap["small_consts"], ap["pool_w"], ap["sinks"], ap["rel_bias"], out_t, scratch, skew, stop=STOP)
    r = run(nc, [{f"in_{n}": v for n, v in arrays.items()}], core_ids=[0])
    o = r.results[0]["out_t"]
    return o.reshape(P, KD, T).transpose(2, 1, 0).reshape(1, T, D)


STOP = None
```
